# Optimizing a Trainium2 kernel written in Bass

```python
import math
import jax, jax.numpy as jnp
from jax import lax
import numpy as np

D_MODEL = 1024
BATCH = 1
SEQ = 512
DEPTH = 2

HEAD_DIM = 64
N_MIXERS = 4
MIX_W = D_MODEL // N_MIXERS
HEADS_PER_MIXER = MIX_W // HEAD_DIM
N_MIX_HEADS = N_MIXERS * HEADS_PER_MIXER
N_IN_PIECES = 11
IN_COLS = N_IN_PIECES * MIX_W
BLOCK = 128
SGU_CHUNK = 128
DILATED_PATTERNS = ((128, 1), (512, 4), (2048, 16))
CONV_WIDTH = 3
PEER_HEADS = 8
PEER_N_KEYS = 128
PEER_N_EXPERTS = PEER_N_KEYS * PEER_N_KEYS
PEER_HALF = 128
PEER_QUERY_DIM = 2 * PEER_HALF
PEER_TOPK = 16
PEER_TOKEN_CHUNK = 128
RMS_EPS = 1e-6
NEG = -1e30

kernel_name = "hybrid_sgu_dilated_conv_stickbreak_peer"

def _rms(x, g):
    xf = x.astype(jnp.float32)
    y = xf * lax.rsqrt(jnp.mean(xf * xf, axis=-1, keepdims=True) + RMS_EPS)
    return (y * g.astype(jnp.float32)).astype(x.dtype)

def _alibi_slopes(n):
    return jnp.asarray(np.array([2.0 ** (-8.0 * (i + 1) / n) for i in range(n)], dtype=np.float32))

def _sgu_mixer(u, v, w_s, b_s, g_v):
    B, S, _ = u.shape
    H, hd, C = HEADS_PER_MIXER, HEAD_DIM, SGU_CHUNK
    u = jax.nn.gelu(u).reshape(B, S, H, hd)
    v = _rms(jax.nn.gelu(v).reshape(B, S, H, hd), g_v.reshape(H, hd))
    v = v.reshape(B, S // C, C, H, hd)
    tril = jnp.tril(jnp.ones((C, C), dtype=bool))
    w = jnp.where(tril[None], w_s, 0.0).astype(v.dtype)
    mixed = jnp.einsum('hts,bcshd->bcthd', w, v) + b_s.T[None, None, :, :, None].astype(v.dtype)
    return (u * mixed.reshape(B, S, H, hd)).reshape(B, S, MIX_W)

def _dilated_pattern(q, k, v, window, dil, slopes):
    B, S, H, hd = q.shape
    L = S // dil
    steps = window // dil
    nb = -(-L // BLOCK)
    Lp = nb * BLOCK

    def to_sub(t):
        return t.reshape(B, L, dil, H, hd).transpose(0, 2, 3, 1, 4)

    pad_q = ((0, 0), (0, 0), (0, 0), (0, Lp - L), (0, 0))
    pad_kv = ((0, 0), (0, 0), (0, 0), (BLOCK, Lp - L), (0, 0))
    qb = jnp.pad(to_sub(q), pad_q).reshape(B, dil, H, nb, BLOCK, hd)
    kb = jnp.pad(to_sub(k), pad_kv).reshape(B, dil, H, nb + 1, BLOCK, hd)
    vb = jnp.pad(to_sub(v), pad_kv).reshape(B, dil, H, nb + 1, BLOCK, hd)
    kband = jnp.concatenate([kb[:, :, :, :-1], kb[:, :, :, 1:]], axis=4)
    vband = jnp.concatenate([vb[:, :, :, :-1], vb[:, :, :, 1:]], axis=4)
    s = jnp.einsum('brhnqd,brhnkd->brhnqk', qb, kband).astype(jnp.float32)
    qi = jnp.arange(BLOCK)
    kj = jnp.arange(2 * BLOCK)
    dist = qi[:, None] + BLOCK - kj[None, :]
    key_pos = jnp.arange(nb)[:, None] * BLOCK - BLOCK + kj[None, :]
    valid = ((dist >= 0) & (dist <= steps))[None] & (key_pos >= 0)[:, None, :]
    s = s - slopes[None, None, :, None, None, None] * (dist * dil).astype(jnp.float32)
    s = jnp.where(valid, s, NEG)
    lse = jax.nn.logsumexp(s, axis=-1)
    p = jnp.exp(s - lse[..., None]).astype(v.dtype)
    o = jnp.einsum('brhnqk,brhnkd->brhnqd', p, vband)
    o = o.reshape(B, dil, H, Lp, hd)[:, :, :, :L].transpose(0, 3, 1, 2, 4).reshape(B, S, H, hd)
    lse = lse.reshape(B, dil, H, Lp)[..., :L].transpose(0, 3, 1, 2).reshape(B, S, H)
    return o, lse

def _dilated_mixer(q, k, v):
    slopes = _alibi_slopes(q.shape[2])
    outs, lses = [], []
    for window, dil in DILATED_PATTERNS:
        o, l = _dilated_pattern(q, k, v, window, dil, slopes)
        outs.append(o)
        lses.append(l)
    w = jax.nn.softmax(jnp.stack(lses, axis=0), axis=0)
    o = jnp.sum(w[..., None].astype(q.dtype) * jnp.stack(outs, axis=0), axis=0)
    return o

def _short_conv_mixer(bg, cg, xt, w):
    y = cg * xt
    y = lax.conv_general_dilated(y, w[:, None, :].astype(y.dtype), window_strides=(1,),
                                 padding=((CONV_WIDTH - 1, 0),),
                                 dimension_numbers=('NWC', 'WIO', 'NWC'),
                                 feature_group_count=MIX_W)
    return bg * y

def _stick_breaking(q, k, v):
    B, S, H, hd = q.shape
    nb = S // BLOCK
    kt = k.transpose(0, 2, 1, 3)
    vt = v.transpose(0, 2, 1, 3)
    qb = q.transpose(0, 2, 1, 3).reshape(B, H, nb, BLOCK, hd).transpose(2, 0, 1, 3, 4)
    spos = jnp.arange(S)

    def block(args):
        qblk, i = args
        z = jnp.einsum('bhqd,bhkd->bhqk', qblk, kt).astype(jnp.float32)
        tpos = i * BLOCK + jnp.arange(BLOCK)
        causal = spos[None, :] < tpos[:, None]
        log_1m = jnp.where(causal, jax.nn.log_sigmoid(-z), 0.0)
        after = lax.cumsum(log_1m, axis=3, reverse=True) - log_1m
        a = jnp.where(causal, jnp.exp(jax.nn.log_sigmoid(z) + after), 0.0)
        return jnp.einsum('bhqk,bhkd->bhqd', a.astype(vt.dtype), vt)

    o = lax.map(block, (qb, jnp.arange(nb)))
    return o.transpose(1, 0, 3, 2, 4).reshape(B, S, H, hd)

def _mixer_block(h, w_in, w_sgu, b_sgu, g_sgu_v, g_q_dil, g_k_dil, conv_w,
                 g_q_sb, g_k_sb, g_head_out, w_out):
    B, S, _ = h.shape
    H, hd = HEADS_PER_MIXER, HEAD_DIM
    scale = HEAD_DIM ** -0.5
    proj = h @ w_in
    (su, sv, dq, dk, dv, cb, cc, cx, bq, bk, bv) = jnp.split(proj, N_IN_PIECES, axis=-1)
    heads = lambda t: t.reshape(B, S, H, hd)
    out_a = _sgu_mixer(su, sv, w_sgu, b_sgu, g_sgu_v)
    qd = _rms(heads(dq), g_q_dil) * scale
    kd = _rms(heads(dk), g_k_dil)
    out_b = _dilated_mixer(qd, kd, heads(dv)).reshape(B, S, MIX_W)
    out_c = _short_conv_mixer(cb, cc, cx, conv_w)
    qs = _rms(heads(bq), g_q_sb) * scale
    ks = _rms(heads(bk), g_k_sb)
    out_d = _stick_breaking(qs, ks, heads(bv)).reshape(B, S, MIX_W)
    cat = jnp.concatenate([out_a, out_b, out_c, out_d], axis=-1).reshape(B, S, N_MIX_HEADS, HEAD_DIM)
    cat = _rms(cat, g_head_out.reshape(N_MIX_HEADS, HEAD_DIM)).reshape(B, S, D_MODEL)
    return cat @ w_out

def _peer(h, w_q, sub_keys, u_tab, v_tab):
    B, S, D = h.shape
    C = PEER_TOKEN_CHUNK
    tok = h.reshape(-1, C, D)

    def chunk(xc):
        q = (xc @ w_q).reshape(C, PEER_HEADS, 2, PEER_HALF)
        s = jnp.einsum('thpd,hpkd->thpk', q, sub_keys).astype(jnp.float32)
        sv, si = lax.top_k(s, PEER_TOPK)
        cand = (sv[:, :, 0, :, None] + sv[:, :, 1, None, :]).reshape(C, PEER_HEADS, PEER_TOPK * PEER_TOPK)
        cidx = (si[:, :, 0, :, None] * PEER_N_KEYS + si[:, :, 1, None, :]).reshape(C, PEER_HEADS, PEER_TOPK * PEER_TOPK)
        top, pos = lax.top_k(cand, PEER_TOPK)
        eidx = jnp.take_along_axis(cidx, pos, axis=-1)
        g = jax.nn.softmax(top, axis=-1)
        a = jnp.einsum('thkd,td->thk', u_tab[eidx], xc).astype(jnp.float32)
        w = (g * jax.nn.gelu(a)).astype(xc.dtype)
        return jnp.einsum('thk,thkd->td', w, v_tab[eidx])

    return lax.map(chunk, tok).reshape(B, S, D)

def setup_inputs(seed: int = 0) -> dict:
    key = jax.random.key(seed)
    ks = jax.random.split(key, 20)
    f32 = jnp.float32
    nrm = lambda k, shape, s: jax.random.normal(k, shape, f32) * s
    gain = lambda k, shape: 1.0 + 0.02 * jax.random.normal(k, shape, f32)
    return {
        "x": jax.random.normal(ks[0], (BATCH, SEQ, D_MODEL), f32),
        "g_mix_norm": gain(ks[1], (DEPTH, D_MODEL)),
        "w_in": nrm(ks[2], (DEPTH, D_MODEL, IN_COLS), D_MODEL ** -0.5),
        "w_sgu": nrm(ks[3], (DEPTH, HEADS_PER_MIXER, SGU_CHUNK, SGU_CHUNK), SGU_CHUNK ** -0.5),
        "b_sgu": gain(ks[4], (DEPTH, HEADS_PER_MIXER, SGU_CHUNK)),
        "g_sgu_v": gain(ks[5], (DEPTH, MIX_W)),
        "g_q_dil": gain(ks[6], (DEPTH, HEAD_DIM)),
        "g_k_dil": gain(ks[7], (DEPTH, HEAD_DIM)),
        "conv_w": nrm(ks[8], (DEPTH, CONV_WIDTH, MIX_W), CONV_WIDTH ** -0.5),
        "g_q_sb": gain(ks[9], (DEPTH, HEAD_DIM)),
        "g_k_sb": gain(ks[10], (DEPTH, HEAD_DIM)),
        "g_head_out": gain(ks[11], (DEPTH, D_MODEL)),
        "w_out": nrm(ks[12], (DEPTH, D_MODEL, D_MODEL), D_MODEL ** -0.5),
        "g_ffn_norm": gain(ks[13], (DEPTH, D_MODEL)),
        "w_peer_q": nrm(ks[14], (DEPTH, D_MODEL, PEER_HEADS * PEER_QUERY_DIM), D_MODEL ** -0.5),
        "peer_sub_keys": nrm(ks[15], (DEPTH, PEER_HEADS, 2, PEER_N_KEYS, PEER_HALF), PEER_HALF ** -0.5),
        "peer_u": nrm(ks[16], (DEPTH, PEER_N_EXPERTS, D_MODEL), D_MODEL ** -0.5),
        "peer_v": nrm(ks[17], (DEPTH, PEER_N_EXPERTS, D_MODEL), PEER_HEADS ** -0.5),
    }

def reference(x, g_mix_norm, w_in, w_sgu, b_sgu, g_sgu_v, g_q_dil, g_k_dil, conv_w,
              g_q_sb, g_k_sb, g_head_out, w_out, g_ffn_norm, w_peer_q, peer_sub_keys,
              peer_u, peer_v):
    for l in range(DEPTH):
        h = _rms(x, g_mix_norm[l])
        x = x + _mixer_block(h, w_in[l], w_sgu[l], b_sgu[l], g_sgu_v[l], g_q_dil[l], g_k_dil[l],
                             conv_w[l], g_q_sb[l], g_k_sb[l], g_head_out[l], w_out[l])
        h = _rms(x, g_ffn_norm[l])
        x = x + _peer(h, w_peer_q[l], peer_sub_keys[l], peer_u[l], peer_v[l])
    return x


_drawn_inputs = setup_inputs


def setup_inputs(seed=0):
    import zlib

    import numpy as np

    out = dict(_drawn_inputs(seed))
    spreads = {}
    factors = {'b_sgu': 4.161,
     'g_sgu_v': 3.565,
     'g_q_dil': 2.987,
     'g_k_dil': 2.895,
     'g_q_sb': 3.794,
     'g_k_sb': 3.767}
    for name, (base, spread) in spreads.items():
        noise = np.random.default_rng([zlib.crc32(name.encode()), seed]).standard_normal(out[name].shape)
        drawn = base * np.exp(spread * noise) if base else spread * noise
        out[name] = __import__('jax').numpy.asarray(drawn.astype(out[name].dtype))
    for name, factor in factors.items():
        out[name] = (out[name] * factor).astype(out[name].dtype)
    return out
```

```python
from contextlib import ExitStack

import numpy as np
import concourse.bass as bass
from concourse import mybir

F32 = mybir.dt.float32
U32 = mybir.dt.uint32
I32 = mybir.dt.int32
ALU = mybir.AluOpType
ACT = mybir.ActivationFunctionType
AX = mybir.AxisListType

P = 128
D = 1024
SEQ = 512
DEPTH = 2
NC = SEQ // P
STEPS = DEPTH * NC
KD = D // P
H, HD = 4, 64
MW = H * HD
PW = 256
N_IN, N_OUT, N_Q = 11, D // PW, 8
PIECES = N_IN + N_OUT + N_Q
PH, TOPK = 8, 16
SLOTS = PH * TOPK
HEADS = STEPS * PH
EPS = 1e-6
NEG = -1e30
LOWEST = -3.0e38
GELU_C = 2.0 * 0.7978845608028654
GELU_A = 0.044715
EXP_CAP = 80.0

IN_ORDER = [2, 3, 8, 9, 4, 10, 0, 1, 5, 6, 7]
DV, BV, SU, SV, CB = 4, 5, 6, 7, 8

NB = 12
NW = 3
ND = 4
BATCHES = 13
(ST_NORM1, ST_IN, ST_QK, ST_DIL, ST_SB, ST_SBPV, ST_SGU, ST_CONV, ST_CAT, ST_OUT, ST_NORM2, ST_TOPK, STAGES) = \
    (0, 1, 7, 8, 12, 16, 17, 18, 19, 20, 21, 22, 30)
SLOTS_PER_STAGE = 4

C_ID, C_TRI, C_ONE, C_BIAS = 0, P, 2 * P, 3 * P
C_MULT = C_BIAS + H * SEQ
C_STRICT = C_MULT + SEQ
C_NEG = C_STRICT + P
C_TRIL = C_NEG + P
C_IOTA = C_TRIL + P
C_EPS = C_IOTA + TOPK
C_WIDTH = C_EPS + 1


def constants():
    c = np.zeros((P, C_WIDTH), np.float32)
    row, col = np.arange(P)[:, None], np.arange(P)[None, :]
    c[:, C_ID:C_ID + P] = row == col
    c[:, C_TRI:C_TRI + P] = row >= col
    c[:, C_ONE:C_ONE + P] = 1.0
    delta = row + (NC - 1) * P - np.arange(SEQ)[None, :]
    mult = ((delta >= 0) & (delta <= 128)).astype(np.float32) + ((delta >= 0) & (delta % 4 == 0)) \
        + ((delta >= 0) & (delta % 16 == 0))
    for h in range(H):
        slope = np.float32(2.0 ** (-8.0 * (h + 1) / H))
        c[:, C_BIAS + h * SEQ:C_BIAS + (h + 1) * SEQ] = np.where(mult > 0, -slope * delta, NEG)
    c[:, C_MULT:C_MULT + SEQ] = mult
    c[:, C_STRICT:C_STRICT + P] = row < col
    c[:, C_NEG:C_NEG + P] = np.where(row < col, 0.0, NEG)
    c[:, C_TRIL:C_TRIL + P] = row <= col
    c[:, C_IOTA:C_IOTA + TOPK] = np.arange(TOPK)
    c[:, C_EPS] = EPS
    return c


def gather_plan():
    plan = []
    for J in range(HEADS + 1):
        for k in range(TOPK):
            if J < HEADS:
                plan.append(("u", J, k))
            if J >= 1:
                plan.append(("v", J - 1, k))
    return plan


def trunk(nc, x_in, cst_in, w_in, w_out, w_q, subkeys, w_sgu, b_sgu, conv_w, g_mix, g_head, g_ffn,
          g_sgu, g_qd, g_kd, g_qs, g_ks, *rest):
    tables_u, tables_v, out = rest[:DEPTH], rest[DEPTH:2 * DEPTH], rest[2 * DEPTH]
    plan = gather_plan()
    at = {g: q for q, g in enumerate(plan)}

    with ExitStack() as ctx:
        def sb(name, shape, dt=F32):
            return ctx.enter_context(nc.sbuf_tensor(name, shape, dt))

        def ps(name, shape):
            return ctx.enter_context(nc.psum_tensor(name, shape, F32))

        def sem(name):
            return ctx.enter_context(nc.semaphore(name))

        x = sb("x", [P, NC, D])
        ring = sb("ring", [P, NB, D])
        wr = sb("wr", [P, NW, KD, PW])
        cst = sb("cst", [P, C_WIDTH])
        gains = sb("gains", [P, 3, D])
        g64 = sb("g64", [P, 4, HD])
        gsv = sb("gsv", [P, MW])
        sgw = sb("sgw", [P, H, P])
        sgb = sb("sgb", [P, H])
        cvw = sb("cvw", [P, 2, 3])
        sub = sb("sub", [P, 2 * PH, P])
        hn = sb("hn", [P, D])
        hT = sb("hT", [P, KD, P])
        htok = sb("htok", [P, 2, D])
        tm = sb("tm", [P, 6, MW])
        fm = sb("fm", [P, 3, 2, P])
        vd = sb("vd", [P, NC, MW])
        vs = sb("vs", [P, NC, MW])
        kdT = sb("kdT", [P, 2, SEQ])
        ksT = sb("ksT", [P, 2, SEQ])
        qdT = sb("qdT", [P, 2, P])
        qsT = sb("qsT", [P, 2, P])
        sq = hn
        cat = sb("cat", [P, 4, MW])
        prob = sb("prob", [P, 2, SEQ])
        probT = sb("probT", [P, 2, SEQ])
        zs, soft = prob, probT
        later = sb("later", [P, SEQ])
        stick = sb("stick", [P, NC, SEQ])
        yc = sb("yc", [P, 2, P + 2])
        cv = sb("cv", [P, 2, P])
        ss = sb("ss", [P, 16])
        rs = sb("rs", [P, 16])
        nt = sb("nt", [P, 2, 16])
        nmax = sb("nmax", [P, H])
        den = sb("den", [P, H])
        rden = sb("rden", [P, H])
        qT = sb("qT", [P, 2, 2, P])
        sc = sb("sc", [P, 2, 2, P])
        sc2 = sb("sc2", [P, 2 * P])
        sv = sb("sv", [P, 2, TOPK])
        si = sb("si", [P, 2, TOPK], U32)
        sif = sb("sif", [P, 2, TOPK])
        cand = sb("cand", [P, TOPK, TOPK])
        top = sb("top", [P, TOPK])
        pos = sb("pos", [P, 3, TOPK], U32)
        posf = sb("posf", [P, 2, TOPK])
        hot = sb("hot", [P, TOPK, TOPK])
        pick = sb("pick", [P, 2, TOPK])
        idx = sb("idx", [P, 2, SLOTS], I32)
        gate = sb("gate", [P, 2, SLOTS])
        gsum = sb("gsum", [P, 2])
        adot = sb("adot", [P, SLOTS])
        gl = sb("gl", [P, TOPK])
        gle = sb("gle", [P, TOPK])
        wgt = sb("wgt", [P, 2, TOPK])
        diag = sb("diag", [P, ND, P])

        psY = ps("psY", [P, D])
        psP = ps("psP", [P, 2, 512])
        psT = ps("psT", [P, 2, 512])
        psS = ps("psS", [P, 512])
        psO = ps("psO", [P, 512])

        ident = cst[:, C_ID:C_ID + P]
        one = cst[:, C_ONE:C_ONE + 1]
        eps = cst[:, C_EPS:C_EPS + 1]

        s_cst = sem("s_cst")
        s_x = [sem(f"s_x{c}") for c in range(NC)]
        s_par = sem("params_loaded")
        w_landed = [sem(f"w_landed{i}") for i in range(NW)]
        g_landed = [sem(f"g_landed{i}") for i in range(NB)]
        piece_used = sem("piece_used")
        piece_ready = sem("piece_ready")
        psp_act = sem("psp_act")
        psp_dve = sem("psp_dve")
        tp_ready = sem("tp_ready")
        tp_taken = sem("tp_taken")
        sumsq = sem("sumsq")
        rough = sem("rough")
        normed = sem("normed")
        qk_done = sem("qk_done")
        scored = sem("scored")
        biased = sem("biased")
        expd = sem("expd")
        weighed = sem("weighed")
        dil_out = sem("dil_out")
        z_half = sem("z_half")
        z_ready = sem("z_ready")
        z_taken = sem("z_taken")
        softed = sem("softed")
        sum_ready = sem("sum_ready")
        lesser = sem("lesser")
        sticked = sem("sticked")
        sb_out = sem("sb_out")
        pso_free = sem("pso_free")
        gated = sem("gated")
        gelu_e = sem("gelu_e")
        sgu_in = sem("sgu_in")
        sgu_out = sem("sgu_out")
        conv_done = sem("conv_done")
        cat_sq = sem("cat_sq")
        x_mixed = sem("x_mixed")
        s_scores = sem("s_scores")
        s_taken = sem("s_taken")
        topped = sem("topped")
        top_exp = sem("top_exp")
        head_done = sem("head_done")
        dotted = sem("dotted")
        a_exp_in = sem("a_exp_in")
        a_exp = sem("a_exp")
        w_ready = sem("w_ready")
        diag_ready = sem("diag_ready")
        v_used = sem("v_used")
        x_done = sem("x_done")
        s_out = sem("s_out")
        dve_chain, act_chain = sem("dve_chain"), sem("act_chain")

        def uses_before(s):
            return sum(t % NC + 1 for t in range(s))

        def pso_use(s, n):
            return uses_before(s) + 3 * s + n

        def psp_freed(G):
            s, i = divmod(G, PIECES)
            d = N_OUT * s + min(max(i + 1 - N_IN, 0), N_OUT)
            if N_IN <= i < N_IN + N_OUT:
                return psp_dve, d
            return psp_act, (PIECES - N_OUT) * s + (i + 1 if i < N_IN else i + 1 - N_OUT)

        block = ctx.enter_context(nc.Block())

        @block.sync
        def _(sp):
            sp.dma_start(cst[:], cst_in).then_inc(s_cst, 16)
            for c in range(NC):
                sp.dma_start(x[:, c], x_in[c * P:(c + 1) * P]).then_inc(s_x[c], 16)
            for s in range(STEPS):
                l, c = divmod(s, NC)
                if c == 0:
                    if l:
                        sp.wait_ge(head_done, PH * s)
                    for i, g in enumerate((g_mix, g_head, g_ffn)):
                        sp.dma_start(gains[:, i], g[l].partition_broadcast(P)).then_inc(s_par, 16)
                    for i, g in enumerate((g_qd, g_kd, g_qs, g_ks)):
                        sp.dma_start(g64[:, i], g[l].partition_broadcast(P)).then_inc(s_par, 16)
                    sp.dma_start(gsv[:], g_sgu[l].partition_broadcast(P)).then_inc(s_par, 16)
                    for t, src in ((sgw, w_sgu), (sgb, b_sgu), (cvw, conv_w), (sub, subkeys)):
                        sp.dma_start(t[:], src[l]).then_inc(s_par, 16)
                for i in range(PIECES):
                    G = PIECES * s + i
                    if G >= NW:
                        sp.wait_ge(piece_used, G - NW + 1)
                    src = w_in[l, i] if i < N_IN else w_out[l, i - N_IN] if i < N_IN + N_OUT else w_q[l, i - N_IN - N_OUT]
                    sp.dma_start(wr[:, G % NW], src).then_inc(w_landed[G % NW], 16)
            for c in range(NC):
                sp.wait_ge(x_done, STEPS - NC + c + 1)
                sp.dma_start(out[c * P:(c + 1) * P], x[:, c]).then_inc(s_out, 16)
            sp.wait_ge(s_out, 16 * NC)

        N_PAR = 12 * 16

        @block.gpsimd
        def _(pool):
            for q, (kind, J, k) in enumerate(plan):
                s, h = divmod(J, PH)
                if kind == "u" and k == 0:
                    pool.wait_ge(head_done, J + 1)
                if q >= NB:
                    k0, J0, i0 = plan[q - NB]
                    pool.wait_ge(dotted if k0 == "u" else v_used, TOPK * J0 + i0 + 1)
                table = (tables_u if kind == "u" else tables_v)[s // NC]
                n = h * TOPK + k
                pool.indirect_dma_start(out=ring[:, q % NB], out_offset=None, in_=table,
                                        in_offset=bass.IndirectOffsetOnAxis(ap=idx[:, s % 2, n:n + 1], axis=0)
                                        ).then_inc(g_landed[q % NB], 16)

        def landed(eng, g):
            q = at[g]
            eng.wait_ge(g_landed[q % NB], 16 * (q // NB + 1))

        @block.scalar
        def _(act):
            made = [0]

            def link(ins):
                made[0] += 1
                ins.then_inc(act_chain, 1)
                act.wait_ge(act_chain, made[0])

            def rough_rsqrt(n, width, terms):
                act.wait_ge(sumsq, n)
                if n >= 2:
                    act.wait_ge(rough, n - 1)
                link(nc.scalar.activation(rs[:, :width], ss[:, :width], ACT.Ln, bias=eps, scale=1.0 / terms))
                nc.scalar.activation(rs[:, :width], rs[:, :width], ACT.Exp, scale=-0.5).then_inc(rough, 1)

            def take_batch(b, dst, width=512):
                act.wait_ge(tp_ready, b + 1)
                nc.scalar.activation(dst, psT[:, b % 2, :width], ACT.Copy).then_inc(tp_taken, 1)

            def row_sumsq(s):
                l, c = divmod(s, NC)
                link(nc.scalar.activation(sq[:], x[:, c], ACT.Square, accum_out=ss[:, 0:1]))
                act.sem_inc(sumsq, 1)

            def take_hT(b, count):
                if b:
                    act.wait_ge(piece_used, count)
                for i in range(2):
                    take_batch(b + i, hT[:, 4 * i:4 * i + 4].rearrange("p a b -> p (a b)"))

            def front(s, stage):
                l, c = divmod(s, NC)
                n = 5 * s
                B = BATCHES * s
                if stage in (ST_NORM1, ST_SGU, ST_NORM2):
                    b = B + {ST_NORM1: 0, ST_SGU: 4, ST_NORM2: 11}[stage]
                    if b:
                        act.wait_ge(tp_ready, b)
                if stage == ST_NORM1:
                    act.wait_ge(s_cst, 16)
                    act.wait_ge(s_x[c], 16)
                    if l:
                        act.wait_ge(x_done, s - NC + 1)
                    if s:
                        act.wait_ge(normed, 3 * s)
                    row_sumsq(s)
                    rough_rsqrt(n + 1, 1, D)
                    take_hT(B, PIECES * s)
                elif ST_IN <= stage < ST_QK:
                    for i in range(2 * (stage - ST_IN), min(2 * (stage - ST_IN) + 2, N_IN)):
                        G = PIECES * s + i
                        act.wait_ge(piece_ready, G + 1)
                        src = psP[:, G % 2, :PW]
                        if i == 0 and s:
                            act.wait_ge(cat_sq, s)
                        if i < 4:
                            dst = tm[:, i]
                        elif i in (DV, BV):
                            dst = (vd if i == DV else vs)[:, c]
                            if l:
                                act.wait_ge(sb_out, s)
                        elif i in (SU, SV):
                            dst = tm[:, 4 + i - SU]
                        else:
                            dst = fm[:, i - CB].rearrange("p a b -> p (a b)")
                        nc.scalar.activation(dst, src, ACT.Copy).then_inc(psp_act, 1)
                elif stage == ST_QK:
                    link(nc.scalar.activation(sq[:], tm[:, 0:4].rearrange("p a b -> p (a b)"), ACT.Square))
                    act.sem_inc(gated, 1)
                    rough_rsqrt(n + 2, 16, HD)
                    for i, (dq, dk) in enumerate(((qdT, kdT), (qsT, ksT))):
                        act.wait_ge(tp_ready, B + 2 + i + 1)
                        v = psT[:, (B + 2 + i) % 2].rearrange("p (a b) -> p a b", a=4)
                        nc.scalar.activation(dq[:], v[:, 0:2], ACT.Copy)
                        nc.scalar.activation(dk[:, :, c * P:(c + 1) * P], v[:, 2:4], ACT.Copy).then_inc(tp_taken, 1)
                elif ST_DIL <= stage < ST_SB:
                    h, w = stage - ST_DIL, (c + 1) * P
                    act.wait_ge(biased, H * s + h + 1)
                    nc.scalar.activation(prob[:, h % 2, :w], prob[:, h % 2, :w], ACT.Exp,
                                         bias=nmax[:, h:h + 1]).then_inc(expd, 1)
                    if h >= 2:
                        act.wait_ge(dil_out, H * s + h - 1)
                    take_batch(B + 4 + h, probT[:, h % 2, :w], w)
                elif ST_SB <= stage < ST_SBPV:
                    i = stage - ST_SB
                    if i > c:
                        return
                    u = uses_before(s) + i
                    act.wait_ge(z_ready, u + 1)
                    if i == 0:
                        act.wait_ge(dil_out, H * (s + 1))
                    if i >= 2:
                        act.wait_ge(sticked, u - 1)
                        act.wait_ge(lesser, u - 1)
                        act.wait_ge(sum_ready, u - 1)
                    link(nc.scalar.activation(soft[:, u % 2], psS[:], ACT.Abs))
                    nc.scalar.activation(zs[:, u % 2], psS[:], ACT.Copy)
                    link(nc.scalar.activation(soft[:, u % 2], soft[:, u % 2], ACT.Exp, scale=-1.0))
                    nc.scalar.activation(soft[:, u % 2], soft[:, u % 2], ACT.Ln, bias=one).then_inc(z_taken, 1)
                    act.wait_ge(lesser, u + 1)
                    if s:
                        act.wait_ge(sb_out, s)
                    nc.scalar.activation(stick[:, c - i], zs[:, u % 2], ACT.Exp).then_inc(sticked, 1)
                elif stage == ST_SGU:
                    act.wait_ge(gated, 3 * s + 2)
                    nc.scalar.activation(sq[:, :2 * MW], sq[:, :2 * MW], ACT.Exp).then_inc(gelu_e, 1)
                    act.wait_ge(gated, 3 * s + 3)
                    link(nc.scalar.activation(sq[:, :MW], tm[:, 5], ACT.Square))
                    act.sem_inc(gelu_e, 1)
                    rough_rsqrt(n + 3, 4, HD)
                elif stage == ST_CONV:
                    take_batch(B + 8, cat[:, 2], MW)
                elif stage == ST_CAT:
                    act.wait_ge(cat_sq, s + 1)
                    link(nc.scalar.activation(sq[:], cat[:].rearrange("p a b -> p (a b)"), ACT.Square))
                    act.sem_inc(gelu_e, 1)
                    rough_rsqrt(n + 4, 16, HD)
                elif stage == ST_OUT:
                    take_hT(B + 9, PIECES * s + N_IN)
                elif stage == ST_NORM2:
                    act.wait_ge(x_mixed, s + 1)
                    row_sumsq(s)
                    rough_rsqrt(n + 5, 1, D)
                    take_hT(B + 11, PIECES * s + N_IN + N_OUT)
                elif stage >= ST_TOPK:
                    h = stage - ST_TOPK
                    T = PH * s + h
                    G = PIECES * s + N_IN + N_OUT + h
                    act.wait_ge(piece_ready, G + 1)
                    if T >= 2:
                        act.wait_ge(s_scores, T - 1)
                        act.wait_ge(head_done, T - 1)
                    nc.scalar.activation(qT[:, T % 2].rearrange("p a b -> p (a b)"), psP[:, G % 2, :PW],
                                         ACT.Copy).then_inc(psp_act, 1)
                    act.wait_ge(s_scores, T + 1)
                    nc.scalar.activation(sc[:, T % 2].rearrange("p a b -> p (a b)"), psS[:, :2 * P],
                                         ACT.Copy).then_inc(s_taken, 1)
                    act.wait_ge(topped, T + 1)
                    nc.scalar.activation(gate[:, s % 2, h * TOPK:(h + 1) * TOPK], top[:], ACT.Exp,
                                         accum_out=gsum[:, 0:1]).then_inc(top_exp, 1)

            for stage in range(STAGES):
                front(0, stage)
            for J in range(HEADS + 1):
                for k in range(TOPK):
                    if J >= 1:
                        m = TOPK * (J - 1) + k
                        if k == 0:
                            act.wait_ge(w_ready, J)
                        if m >= ND:
                            act.wait_ge(v_used, m - ND + 1)
                        nc.scalar.activation(diag[:, m % ND], ident, ACT.Copy,
                                             scale=wgt[:, (J - 1) % 2, k:k + 1]).then_inc(diag_ready, 1)
                    slot = J % PH * TOPK + k
                    if J + PH < HEADS and slot % SLOTS_PER_STAGE == 0 and slot // SLOTS_PER_STAGE < STAGES:
                        front(J // PH + 1, slot // SLOTS_PER_STAGE)
                if J < HEADS:
                    act.wait_ge(a_exp_in, J + 1)
                    nc.scalar.activation(gle[:], gle[:], ACT.Exp).then_inc(a_exp, 1)

        @block.tensor
        def _(pe):
            def transposes(b, srcs):
                if b >= 2:
                    pe.wait_ge(tp_taken, b - 1)
                for i, src in enumerate(srcs):
                    last = nc.tensor.transpose(psT[:, b % 2, i * P:(i + 1) * P], src, ident)
                last.then_inc(tp_ready, 1)

            def project(s, i):
                G = PIECES * s + i
                pe.wait_ge(w_landed[G % NW], 16 * (G // NW + 1))
                if G >= 2:
                    pe.wait_ge(*psp_freed(G - 2))
                w = wr[:, G % NW]
                if CB <= i < N_IN or i >= N_IN + N_OUT:
                    for b in range(2):
                        for k in range(KD):
                            last = nc.tensor.matmul(psP[:, G % 2, b * P:(b + 1) * P], w[:, k, b * P:(b + 1) * P],
                                                    hT[:, k], start=(k == 0), stop=(k == KD - 1))
                else:
                    for k in range(KD):
                        last = nc.tensor.matmul(psP[:, G % 2, :PW], hT[:, k], w[:, k], start=(k == 0), stop=(k == KD - 1))
                last.then_inc(piece_ready, 1)
                pe.wait_ge(piece_ready, G + 1)
                pe.sem_inc(piece_used, 1)

            def score(s, h):
                l, c = divmod(s, NC)
                if h == 0:
                    pe.wait_ge(tp_taken, BATCHES * s + 4)
                    if s:
                        pe.wait_ge(s_taken, PH * s)
                else:
                    pe.wait_ge(biased, H * s + h)
                r = slice(HD * (h % 2), HD * (h % 2) + HD)
                nc.tensor.matmul(psS[:, :(c + 1) * P], qdT[r, h // 2], kdT[r, h // 2, :(c + 1) * P],
                                 start=True, stop=True).then_inc(scored, 1)

            def logits(s, i):
                l, c = divmod(s, NC)
                u = uses_before(s) + i
                if i == 0:
                    pe.wait_ge(biased, H * (s + 1))
                else:
                    pe.wait_ge(z_taken, u)
                kc = c - i
                for h in (0, 2, 1, 3):
                    if h == 1:
                        last.then_inc(z_half, 1)
                        pe.wait_ge(z_half, u + 1)
                    r = slice(HD * (h % 2), HD * (h % 2) + HD)
                    last = nc.tensor.matmul(psS[:, h * P:(h + 1) * P], ksT[r, h // 2, kc * P:(kc + 1) * P],
                                            qsT[r, h // 2], start=True, stop=True)
                last.then_inc(z_ready, 1)

            def pso_wait(s, n):
                if pso_use(s, n):
                    pe.wait_ge(pso_free, pso_use(s, n))

            def front(s, stage):
                l, c = divmod(s, NC)
                B = BATCHES * s
                if stage in (ST_NORM1, ST_OUT, ST_NORM2):
                    n, b = {ST_NORM1: (1, 0), ST_OUT: (2, 9), ST_NORM2: (3, 11)}[stage]
                    pe.wait_ge(normed, 3 * s + n)
                    for i in range(2):
                        transposes(B + b + i, [hn[:, (4 * i + j) * P:(4 * i + j + 1) * P] for j in range(4)])
                    pe.wait_ge(tp_taken, B + b + 2)
                    if stage == ST_OUT:
                        for i in range(N_OUT):
                            project(s, N_IN + i)
                elif ST_IN <= stage < ST_QK:
                    for i in range(2 * (stage - ST_IN), min(2 * (stage - ST_IN) + 2, N_IN)):
                        project(s, i)
                elif stage == ST_QK:
                    pe.wait_ge(qk_done, s + 1)
                    for i in range(2):
                        transposes(B + 2 + i, [hn[:, (4 * i + j) * P:(4 * i + j + 1) * P] for j in range(4)])
                elif ST_DIL <= stage < ST_SB:
                    h = stage - ST_DIL
                    if h == 0:
                        score(s, 0)
                    if h + 1 < H:
                        score(s, h + 1)
                    pe.wait_ge(weighed, H * s + h + 1)
                    transposes(B + 4 + h, [prob[:, h % 2, j * P:(j + 1) * P] for j in range(c + 1)])
                    pe.wait_ge(tp_taken, B + 4 + h + 1)
                    if h == 0:
                        pso_wait(s, 0)
                    for j in range(c + 1):
                        last = nc.tensor.matmul(psO[:, h * HD:(h + 1) * HD], probT[:, h % 2, j * P:(j + 1) * P],
                                                vd[:, j, h * HD:(h + 1) * HD], start=(j == 0), stop=(j == c))
                    last.then_inc(dil_out, 1)
                elif ST_SB <= stage < ST_SBPV:
                    i = stage - ST_SB
                    if i > c:
                        return
                    u = uses_before(s) + i
                    if i == 0:
                        logits(s, 0)
                    if i < c:
                        logits(s, i + 1)
                    pe.wait_ge(softed, u + 1)
                    pso_wait(s, 1 + i)
                    last = nc.tensor.matmul(psO[:], cst[:, C_TRI:C_TRI + P], soft[:, u % 2], start=True, stop=(i == 0))
                    if i:
                        last = nc.tensor.matmul(psO[:], cst[:, C_ONE:C_ONE + P], later[:], start=False, stop=True)
                    last.then_inc(sum_ready, 1)
                elif stage == ST_SBPV:
                    pe.wait_ge(sticked, uses_before(s + 1))
                    pso_wait(s, c + 2)
                    for h in range(H):
                        for j in range(c + 1):
                            last = nc.tensor.matmul(psO[:, h * HD:(h + 1) * HD], stick[:, j, h * P:(h + 1) * P],
                                                    vs[:, j, h * HD:(h + 1) * HD], start=(j == 0), stop=(j == c))
                    last.then_inc(sb_out, 1)
                elif stage == ST_SGU:
                    pe.wait_ge(sgu_in, s + 1)
                    pso_wait(s, c + 3)
                    for h in range(H):
                        last = nc.tensor.matmul(psO[:, h * HD:(h + 1) * HD], sgw[:, h], tm[:, 5, h * HD:(h + 1) * HD],
                                                start=True, stop=True)
                    last.then_inc(sgu_out, 1)
                elif stage == ST_CONV:
                    pe.wait_ge(conv_done, s + 1)
                    transposes(B + 8, [cv[:, 0], cv[:, 1]])
                elif stage >= ST_TOPK:
                    h = stage - ST_TOPK
                    T = PH * s + h
                    project(s, N_IN + N_OUT + h)
                    pe.wait_ge(*psp_freed(PIECES * s + N_IN + N_OUT + h))
                    if h == 0:
                        pe.wait_ge(z_taken, uses_before(s + 1))
                    else:
                        pe.wait_ge(s_taken, T)
                    for b in range(2):
                        last = nc.tensor.matmul(psS[:, b * P:(b + 1) * P], qT[:, T % 2, b], sub[:, 2 * h + b],
                                                start=True, stop=True)
                    last.then_inc(s_scores, 1)

            pe.wait_ge(s_cst, 16)
            pe.wait_ge(s_par, N_PAR)
            for stage in range(STAGES):
                front(0, stage)
            for J in range(HEADS + 1):
                for k in range(TOPK):
                    if J >= 1:
                        s, h = divmod(J - 1, PH)
                        n = h * TOPK + k
                        landed(pe, ("v", J - 1, k))
                        pe.wait_ge(diag_ready, TOPK * (J - 1) + k + 1)
                        if n == 0 and s:
                            pe.wait_ge(x_done, s)
                        r = ring[:, at[("v", J - 1, k)] % NB]
                        for b in range(2):
                            last = nc.tensor.matmul(psY[:, b * 512:(b + 1) * 512], diag[:, (TOPK * (J - 1) + k) % ND],
                                                    r[:, b * 512:(b + 1) * 512], start=(n == 0), stop=(n == SLOTS - 1))
                        last.then_inc(v_used, 1)
                    slot = J % PH * TOPK + k
                    if J + PH < HEADS and slot % SLOTS_PER_STAGE == 0 and slot // SLOTS_PER_STAGE < STAGES:
                        if slot == 0 and (J // PH + 1) % NC == 0:
                            pe.wait_ge(s_par, N_PAR * ((J // PH + 1) // NC + 1))
                        front(J // PH + 1, slot // SLOTS_PER_STAGE)

        @block.vector
        def _(dve):
            v = nc.vector
            made = [0]

            def link(ins):
                made[0] += 1
                ins.then_inc(dve_chain, 1)
                dve.wait_ge(dve_chain, made[0])

            def sharpen(n, width, terms):
                m, r, t, u = ss[:, :width], rs[:, :width], nt[:, 0, :width], nt[:, 1, :width]
                link(v.tensor_scalar(t, m, 1.0 / terms, EPS, ALU.mult, ALU.add))
                dve.wait_ge(rough, n)
                link(v.tensor_tensor(u, r, r, ALU.mult))
                link(v.tensor_tensor(u, u, t, ALU.mult))
                link(v.tensor_scalar(u, u, -0.5, 1.5, ALU.mult, ALU.add))
                link(v.tensor_tensor(r, r, u, ALU.mult))

            def gelu_exponent(dst, tmp, src):
                link(v.tensor_tensor(tmp, src, src, ALU.mult))
                link(v.tensor_scalar(tmp, tmp, -GELU_C * GELU_A, -GELU_C, ALU.mult, ALU.add))
                link(v.tensor_tensor(tmp, tmp, src, ALU.mult))

            def per_head(t, heads):
                return t[:, :heads].unsqueeze(2).broadcast_to([P, heads, HD])

            def top16(src, values, places, width):
                link(v.max(values[:, 0:8], src))
                link(v.max_index(places[:, 0:8], values[:, 0:8], src))
                link(v.match_replace(sc2[:, :width], values[:, 0:8], src, LOWEST))
                link(v.max(values[:, 8:16], sc2[:, :width]))
                link(v.max_index(places[:, 8:16], values[:, 8:16], sc2[:, :width]))

            def front(s, stage):
                l, c = divmod(s, NC)
                n = 5 * s
                if stage == ST_NORM1:
                    if s:
                        dve.wait_ge(tp_ready, BATCHES * s)
                    dve.wait_ge(sumsq, n + 1)
                    sharpen(n + 1, 1, D)
                    v.scalar_tensor_tensor(out=hn[:], in0=x[:, c], scalar=rs[:, 0:1], in1=gains[:, 0],
                                           op0=ALU.mult, op1=ALU.mult).then_inc(normed, 1)
                elif stage == ST_QK:
                    dve.wait_ge(gated, 3 * s + 1)
                    v.tensor_reduce(ss[:], sq[:].rearrange("p (h d) -> p h d", d=HD), AX.X, ALU.add).then_inc(sumsq, 1)
                    dve.wait_ge(sumsq, n + 2)
                    sharpen(n + 2, 16, HD)
                    dve.wait_ge(tp_ready, BATCHES * s + 2)
                    hv = hn[:].rearrange("p (h d) -> p h d", d=HD)
                    link(v.tensor_tensor(hv, tm[:, 0:4].rearrange("p a (h d) -> p (a h) d", d=HD), per_head(rs, 16), ALU.mult))
                    h4 = hn[:].rearrange("p (a h d) -> p a h d", a=4, d=HD)
                    link(v.tensor_tensor(h4, h4, g64[:].unsqueeze(2).broadcast_to([P, 4, H, HD]), ALU.mult))
                    q = hn[:].rearrange("p (a b c) -> p a b c", a=2, b=2)[:, :, 0]
                    v.tensor_scalar(q, q, HD ** -0.5, None, ALU.mult).then_inc(qk_done, 1)
                elif ST_DIL <= stage < ST_SB:
                    h, w = stage - ST_DIL, (c + 1) * P
                    N = H * s + h
                    pr = prob[:, h % 2, :w]
                    o = C_BIAS + h * SEQ + (NC - 1 - c) * P
                    if h == 0 and s:
                        dve.wait_ge(sb_out, s)
                    if h >= 2:
                        dve.wait_ge(tp_ready, BATCHES * s + 4 + h - 1)
                    dve.wait_ge(scored, N + 1)
                    link(v.tensor_tensor(pr, psS[:, :w], cst[:, o:o + w], ALU.add))
                    v.tensor_reduce(nmax[:, h:h + 1], pr, AX.X, ALU.max, negate=True).then_inc(biased, 1)
                    dve.wait_ge(expd, N + 1)
                    o = C_MULT + (NC - 1 - c) * P
                    v.tensor_tensor_reduce(out=pr, in0=pr, in1=cst[:, o:o + w], scale=1.0, scalar=0.0, op0=ALU.mult,
                                           op1=ALU.add, accum_out=den[:, h:h + 1]).then_inc(weighed, 1)
                    if h == H - 1:
                        dve.wait_ge(weighed, N + 1)
                        link(v.reciprocal(rden[:], den[:]))
                        dve.wait_ge(dil_out, N + 1)
                        if s:
                            dve.wait_ge(gelu_e, 3 * s)
                        v.tensor_tensor(cat[:, 1].rearrange("p (h d) -> p h d", d=HD),
                                        psO[:, :MW].rearrange("p (h d) -> p h d", d=HD), per_head(rden, H),
                                        ALU.mult).then_inc(pso_free, 1)
                elif ST_SB <= stage < ST_SBPV:
                    i = stage - ST_SB
                    if i > c:
                        return
                    u = uses_before(s) + i
                    z, f = zs[:, u % 2], soft[:, u % 2]
                    dve.wait_ge(z_taken, u + 1)
                    if i == 1:
                        link(v.tensor_copy(later[:], soft[:, (u - 1) % 2]))
                    elif i > 1:
                        dve.wait_ge(sum_ready, u)
                        link(v.tensor_tensor(later[:], later[:], soft[:, (u - 1) % 2], ALU.add))
                    def masked(t):
                        return t.rearrange("p (h q) -> p h q", q=P)
                    def mask(o):
                        return cst[:, o:o + P].unsqueeze(1).broadcast_to([P, H, P])
                    ins = v.scalar_tensor_tensor(out=f, in0=z, scalar=0.0, in1=f, op0=ALU.max, op1=ALU.add)
                    if i == 0:
                        link(ins)
                        ins = v.tensor_tensor(masked(f), masked(f), mask(C_STRICT), ALU.mult)
                    ins.then_inc(softed, 1)
                    dve.wait_ge(sum_ready, u + 1)
                    link(v.tensor_tensor(z, z, psO[:], ALU.subtract))
                    if i == 0:
                        link(v.tensor_scalar(z, z, 0.0, None, ALU.min))
                        v.tensor_tensor(masked(z), masked(z), mask(C_NEG), ALU.add).then_inc(lesser, 1)
                    else:
                        v.tensor_scalar(z, z, 0.0, None, ALU.min).then_inc(lesser, 1)
                    dve.wait_ge(lesser, u + 1)
                    dve.sem_inc(pso_free, 1)
                elif stage == ST_SBPV:
                    dve.wait_ge(sb_out, s + 1)
                    v.tensor_copy(cat[:, 3], psO[:, :MW]).then_inc(pso_free, 1)
                elif stage == ST_SGU:
                    uv = tm[:, 4:6].rearrange("p a b -> p (a b)")
                    e = sq[:, :2 * MW]
                    dve.wait_ge(qk_done, s + 1)
                    gelu_exponent(None, e, uv)
                    v.tensor_scalar(e, e, EXP_CAP, None, ALU.min).then_inc(gated, 1)
                    dve.wait_ge(gelu_e, 3 * s + 1)
                    link(v.tensor_scalar(e, e, 1.0, None, ALU.add))
                    link(v.reciprocal(e, e))
                    v.tensor_tensor(uv, uv, e, ALU.mult).then_inc(gated, 1)
                    if c == 0:
                        link(v.tensor_tensor(sgw[:], sgw[:], cst[:, C_TRIL:C_TRIL + P].unsqueeze(1).broadcast_to([P, H, P]), ALU.mult))
                    dve.wait_ge(gelu_e, 3 * s + 2)
                    v.tensor_reduce(ss[:, :H], sq[:, :MW].rearrange("p (h d) -> p h d", d=HD), AX.X, ALU.add).then_inc(sumsq, 1)
                    dve.wait_ge(sumsq, n + 3)
                    sharpen(n + 3, H, HD)
                    vv = tm[:, 5].rearrange("p (h d) -> p h d", d=HD)
                    link(v.tensor_tensor(vv, vv, per_head(rs, H), ALU.mult))
                    v.tensor_tensor(tm[:, 5], tm[:, 5], gsv[:], ALU.mult).then_inc(sgu_in, 1)
                    dve.wait_ge(sgu_out, s + 1)
                    for h in range(H):
                        o = slice(h * HD, (h + 1) * HD)
                        last = v.scalar_tensor_tensor(out=cat[:, 0, o], in0=psO[:, o], scalar=sgb[:, h:h + 1],
                                                      in1=tm[:, 4, o], op0=ALU.add, op1=ALU.mult)
                    last.then_inc(pso_free, 1)
                elif stage == ST_CONV:
                    if c == 0:
                        link(v.memset(yc[:, :, 0:2], 0.0))
                    else:
                        link(v.tensor_copy(yc[:, :, 0:2], yc[:, :, P:P + 2]))
                    link(v.tensor_tensor(yc[:, :, 2:], fm[:, 1], fm[:, 2], ALU.mult))
                    if s:
                        dve.wait_ge(tp_ready, BATCHES * (s - 1) + 9)
                    for b in range(2):
                        link(v.tensor_scalar(cv[:, b], yc[:, b, 0:P], cvw[:, b, 0:1], None, ALU.mult))
                        for t in (1, 2):
                            link(v.scalar_tensor_tensor(out=cv[:, b], in0=yc[:, b, t:t + P], scalar=cvw[:, b, t:t + 1],
                                                        in1=cv[:, b], op0=ALU.mult, op1=ALU.add))
                    v.tensor_tensor(cv[:], cv[:], fm[:, 0], ALU.mult).then_inc(conv_done, 1)
                elif stage == ST_CAT:
                    dve.wait_ge(tp_taken, BATCHES * s + 9)
                    dve.wait_ge(pso_free, pso_use(s + 1, 0))
                    dve.sem_inc(cat_sq, 1)
                    dve.wait_ge(gelu_e, 3 * s + 3)
                    v.tensor_reduce(ss[:], sq[:].rearrange("p (h d) -> p h d", d=HD), AX.X, ALU.add).then_inc(sumsq, 1)
                    dve.wait_ge(sumsq, n + 4)
                    sharpen(n + 4, 16, HD)
                    dve.wait_ge(tp_ready, BATCHES * s + 4)
                    hv = hn[:].rearrange("p (h d) -> p h d", d=HD)
                    link(v.tensor_tensor(hv, cat[:].rearrange("p a (h d) -> p (a h) d", d=HD), per_head(rs, 16), ALU.mult))
                    v.tensor_tensor(hn[:], hn[:], gains[:, 1], ALU.mult).then_inc(normed, 1)
                elif stage == ST_OUT:
                    for i in range(N_OUT):
                        G = PIECES * s + N_IN + i
                        dve.wait_ge(piece_ready, G + 1)
                        xs = x[:, c, i * PW:(i + 1) * PW]
                        v.tensor_tensor(xs, xs, psP[:, G % 2, :PW], ALU.add).then_inc(psp_dve, 1)
                    dve.wait_ge(psp_dve, N_OUT * (s + 1))
                    dve.sem_inc(x_mixed, 1)
                elif stage == ST_NORM2:
                    dve.wait_ge(sumsq, n + 5)
                    sharpen(n + 5, 1, D)
                    if s >= 2:
                        dve.wait_ge(dotted, SLOTS * (s - 1))
                    link(v.scalar_tensor_tensor(out=htok[:, s % 2], in0=x[:, c], scalar=rs[:, 0:1], in1=gains[:, 2],
                                                op0=ALU.mult, op1=ALU.mult))
                    dve.wait_ge(tp_ready, BATCHES * s + 11)
                    v.tensor_copy(hn[:], htok[:, s % 2]).then_inc(normed, 1)
                elif stage >= ST_TOPK:
                    h = stage - ST_TOPK
                    T = PH * s + h
                    if h == 0 and s >= 2:
                        dve.wait_ge(v_used, SLOTS * (s - 1))
                    dve.wait_ge(s_taken, T + 1)
                    for b in range(2):
                        top16(sc[:, T % 2, b], sv[:, b], si[:, b], P)
                    link(v.tensor_tensor(cand[:], sv[:, 0].unsqueeze(2).broadcast_to([P, TOPK, TOPK]),
                                         sv[:, 1].unsqueeze(1).broadcast_to([P, TOPK, TOPK]), ALU.add))
                    if T:
                        dve.wait_ge(top_exp, T)
                    top16(cand[:].rearrange("p a b -> p (a b)"), top, pos[:, 0], TOPK * TOPK)
                    link(v.tensor_scalar(gsum[:, 1:2], top[:, 0:1], 1.0, None, ALU.mult))
                    v.tensor_scalar(top[:], top[:], gsum[:, 1:2], None, ALU.subtract).then_inc(topped, 1)
                    link(v.tensor_copy(sif[:], si[:]))
                    link(v.tensor_scalar(pos[:, 1], pos[:, 0], 4, None, ALU.logical_shift_right))
                    link(v.tensor_scalar(pos[:, 2], pos[:, 0], 15, None, ALU.bitwise_and))
                    link(v.tensor_copy(posf[:], pos[:, 1:3]))
                    for b in range(2):
                        link(v.tensor_tensor(hot[:], posf[:, b].unsqueeze(2).broadcast_to([P, TOPK, TOPK]),
                                             cst[:, C_IOTA:C_IOTA + TOPK].unsqueeze(1).broadcast_to([P, TOPK, TOPK]), ALU.is_equal))
                        link(v.tensor_tensor(hot[:], hot[:], sif[:, b].unsqueeze(1).broadcast_to([P, TOPK, TOPK]), ALU.mult))
                        link(v.tensor_reduce(pick[:, b], hot[:], AX.X, ALU.add))
                    o = slice(h * TOPK, (h + 1) * TOPK)
                    link(v.scalar_tensor_tensor(out=idx[:, s % 2, o], in0=pick[:, 0], scalar=float(P), in1=pick[:, 1],
                                                op0=ALU.mult, op1=ALU.add))
                    dve.wait_ge(top_exp, T + 1)
                    link(v.reciprocal(gsum[:, 1:2], gsum[:, 0:1]))
                    g = gate[:, s % 2, o]
                    v.tensor_scalar(g, g, gsum[:, 1:2], None, ALU.mult).then_inc(head_done, 1)

            def add_peer(s):
                dve.wait_ge(v_used, SLOTS * (s + 1))
                v.tensor_tensor(x[:, s % NC], x[:, s % NC], psY[:], ALU.add).then_inc(x_done, 1)

            dve.wait_ge(s_cst, 16)
            dve.wait_ge(s_par, N_PAR)
            for stage in range(STAGES):
                front(0, stage)
            for J in range(HEADS + 1):
                s, h = divmod(J, PH)
                for k in range(TOPK):
                    if J < HEADS:
                        n = h * TOPK + k
                        landed(dve, ("u", J, k))
                        if n == 0:
                            dve.wait_ge(head_done, J + 1)
                        r = ring[:, at[("u", J, k)] % NB]
                        v.tensor_tensor_reduce(out=r, in0=r, in1=htok[:, s % 2], scale=1.0, scalar=0.0,
                                               op0=ALU.mult, op1=ALU.add, accum_out=adot[:, n:n + 1]).then_inc(dotted, 1)
                    slot = h * TOPK + k
                    if J + PH < HEADS and slot % SLOTS_PER_STAGE == 0 and slot // SLOTS_PER_STAGE < STAGES:
                        if slot == 0 and (s + 1) % NC == 0:
                            dve.wait_ge(s_par, N_PAR * ((s + 1) // NC + 1))
                        front(s + 1, slot // SLOTS_PER_STAGE)
                if J < HEADS:
                    a = adot[:, h * TOPK:(h + 1) * TOPK]
                    dve.wait_ge(dotted, TOPK * (J + 1))
                    gelu_exponent(None, gl[:], a)
                    v.tensor_scalar(gle[:], gl[:], EXP_CAP, None, ALU.min).then_inc(a_exp_in, 1)
                    dve.wait_ge(a_exp, J + 1)
                    link(v.tensor_scalar(gl[:], gle[:], 1.0, None, ALU.add))
                    link(v.reciprocal(gl[:], gl[:]))
                    link(v.tensor_tensor(gl[:], gl[:], a, ALU.mult))
                    if J >= 2:
                        dve.wait_ge(diag_ready, TOPK * (J - 1))
                    v.tensor_tensor(wgt[:, J % 2], gl[:], gate[:, s % 2, h * TOPK:(h + 1) * TOPK], ALU.mult).then_inc(w_ready, 1)
                if J >= PH and J % PH == 0:
                    add_peer(J // PH - 1)


def kernel(x, g_mix_norm, w_in, w_sgu, b_sgu, g_sgu_v, g_q_dil, g_k_dil, conv_w, g_q_sb, g_k_sb, g_head_out,
           w_out, g_ffn_norm, w_peer_q, peer_sub_keys, peer_u, peer_v):
    import concourse.bacc as bacc
    from concourse.bass_utils import run_bass_kernel_spmd

    def pieces(w):
        w = np.asarray(w)
        return w.reshape(DEPTH, KD, P, -1, PW).transpose(0, 3, 2, 1, 4)

    ins = {
        "x": np.asarray(x).reshape(SEQ, D),
        "cst": constants(),
        "w_in": pieces(w_in)[:, IN_ORDER],
        "w_out": pieces(w_out),
        "w_q": pieces(w_peer_q),
        "subkeys": np.asarray(peer_sub_keys).reshape(DEPTH, 2 * PH, P, P).transpose(0, 3, 1, 2),
        "w_sgu": np.asarray(w_sgu).transpose(0, 3, 1, 2),
        "b_sgu": np.asarray(b_sgu).transpose(0, 2, 1),
        "conv_w": np.asarray(conv_w).reshape(DEPTH, 3, 2, P).transpose(0, 3, 2, 1),
        "g_mix": np.asarray(g_mix_norm), "g_head": np.asarray(g_head_out), "g_ffn": np.asarray(g_ffn_norm),
        "g_sgu": np.asarray(g_sgu_v), "g_qd": np.asarray(g_q_dil), "g_kd": np.asarray(g_k_dil),
        "g_qs": np.asarray(g_q_sb), "g_ks": np.asarray(g_k_sb),
        "u0": np.asarray(peer_u)[0], "u1": np.asarray(peer_u)[1],
        "v0": np.asarray(peer_v)[0], "v1": np.asarray(peer_v)[1],
    }
    nc = bacc.Bacc("TRN2", target_bir_lowering=False, num_devices=1)
    arrays, args = {}, []
    for name, a in ins.items():
        a = np.ascontiguousarray(a)
        arrays["in_" + name] = a
        args.append(nc.dram_tensor("in_" + name, a.shape, mybir.dt.from_np(a.dtype), kind="ExternalInput").ap())
    args.append(nc.dram_tensor("out", (SEQ, D), F32, kind="ExternalOutput").ap())
    trunk(nc, *args)
    r = run_bass_kernel_spmd(nc, [arrays], core_ids=[0])
    return r.results[0]["out"].reshape(1, SEQ, D)
```

```python
from contextlib import ExitStack

import numpy as np
import concourse.bass as bass
from concourse import mybir

F32 = mybir.dt.float32
U32 = mybir.dt.uint32
I32 = mybir.dt.int32
ALU = mybir.AluOpType
ACT = mybir.ActivationFunctionType
AX = mybir.AxisListType

P = 128
D = 1024
SEQ = 512
DEPTH = 2
NC = SEQ // P
STEPS = DEPTH * NC
KD = D // P
H, HD = 4, 64
MW = H * HD
PW = 256
N_IN, N_OUT, N_Q = 11, D // PW, 8
PIECES = N_IN + N_OUT + N_Q
PH, TOPK = 8, 16
SLOTS = PH * TOPK
PE_K = [k for k in range(TOPK) if k % 4 != 3]
DVE_K = [k for k in range(TOPK) if k % 4 == 3]
HEADS = STEPS * PH
EPS = 1e-6
NEG = -1e30
LOWEST = -3.0e38
GELU_C = 2.0 * 0.7978845608028654
GELU_A = 0.044715
EXP_CAP = 80.0

IN_ORDER = [2, 3, 8, 9, 4, 10, 0, 1, 5, 6, 7]
DV, BV, SU, SV, CB = 4, 5, 6, 7, 8

NB = 12
NW = 3
ND = 4
BATCHES = 13

PIECE_AT, DIL_AT, STICK_AT, OUT_AT, TOP_AT = 4, 20, 40, 73, 82
ACT_PARTS = [(0, "norm1", 0), (3, "hT1", 0), (12, "qk squares", 0), (14, "qk root", 0), (18, "qk taken", 0),
             (28, "gelu exp", 0), (30, "v squares", 0), (32, "v root", 0), (39, "conv taken", 0),
             (66, "cat squares", 0), (68, "cat root", 0), (72, "catT", 0), (78, "norm2", 0), (81, "hT2", 0),
             (124, "gate exp", 0)]
ACT_PARTS += [(PIECE_AT + 1 + 2 * i, "piece", i) for i in range(N_IN)]
ACT_PARTS += [(DIL_AT + 2 + 4 * h, "dil exp", h) for h in range(H)]
ACT_PARTS += [(DIL_AT + 5 + 4 * h, "dil taken", h) for h in range(H)]
ACT_PARTS += [(STICK_AT + 1 + 6 * i, "logits", i) for i in range(NC)]
ACT_PARTS += [(STICK_AT + 5 + 6 * i, "stick exp", i) for i in range(NC)]
ACT_PARTS += [(TOP_AT + 1 + 5 * h, "queries", h) for h in range(PH)]
ACT_PARTS += [(TOP_AT + 2 + 5 * h, "key scores", h) for h in range(PH)]
PE_PARTS = [(2, "hT1", 0), (17, "qk", 0), (38, "conv", 0), (41, "sgu", 0), (64, "stick out", 0), (71, "catT", 0),
            (80, "hT2", 0)]
PE_PARTS += [(PIECE_AT + 2 * i, "piece", i) for i in range(N_IN)]
PE_PARTS += [(DIL_AT + 4 * h, "scores", h) for h in range(H)]
PE_PARTS += [(DIL_AT + 4 + 4 * h, "dil T", h) for h in range(H)]
PE_PARTS += [(DIL_AT + 6 + 4 * h, "dil out", h) for h in range(H)]
PE_PARTS += [(STICK_AT + 6 * i, "logits", i) for i in range(NC)]
PE_PARTS += [(STICK_AT + 3 + 6 * i, "sums", i) for i in range(NC)]
PE_PARTS += [(OUT_AT + i, "piece", N_IN + i) for i in range(N_OUT)]
PE_PARTS += [(TOP_AT + 5 * h, "piece", N_IN + N_OUT + h) for h in range(PH)]
PE_PARTS += [(TOP_AT + 2 + 5 * h, "key scores", h) for h in range(PH)]
DVE_PARTS = [(1, "norm1", 0), (13, "qk sums", 0), (15, "qk", 0), (27, "gelu in", 0), (29, "gelu", 0),
             (31, "v sums", 0), (33, "sgu in", 0), (35, "conv", 0), (39, "dil out", 0), (42, "sgu", 0), (65, "stick out", 0),
             (67, "cat sums", 0), (69, "cat", 0), (79, "norm2", 0), (125, "gate", 0)]
DVE_PARTS += [(DIL_AT + 1 + 4 * h, "bias", h) for h in range(H)]
DVE_PARTS += [(DIL_AT + 3 + 4 * h, "weigh", h) for h in range(H)]
DVE_PARTS += [(STICK_AT + 2 + 6 * i, "softplus", i) for i in range(NC)]
DVE_PARTS += [(STICK_AT + 4 + 6 * i, "exponent", i) for i in range(NC)]
DVE_PARTS += [(OUT_AT + 1 + i, "out", i) for i in range(N_OUT)]
DVE_PARTS += [(TOP_AT + 3 + 5 * h, "top keys", h) for h in range(PH)]
DVE_PARTS += [(TOP_AT + 4 + 5 * h, "top pairs", h) for h in range(PH)]


def at_slot(parts, slot):
    return [(part, n) for at, part, n in parts if at == slot]


C_ID, C_TRI, C_ONE, C_BIAS = 0, P, 2 * P, 3 * P
C_MULT = C_BIAS + H * SEQ
C_STRICT = C_MULT + SEQ
C_NEG = C_STRICT + P
C_TRIL = C_NEG + P
C_IOTA = C_TRIL + P
C_EPS = C_IOTA + TOPK
C_WIDTH = C_EPS + 1


def constants():
    c = np.zeros((P, C_WIDTH), np.float32)
    row, col = np.arange(P)[:, None], np.arange(P)[None, :]
    c[:, C_ID:C_ID + P] = row == col
    c[:, C_TRI:C_TRI + P] = row >= col
    c[:, C_ONE:C_ONE + P] = 1.0
    delta = row + (NC - 1) * P - np.arange(SEQ)[None, :]
    mult = ((delta >= 0) & (delta <= 128)).astype(np.float32) + ((delta >= 0) & (delta % 4 == 0)) \
        + ((delta >= 0) & (delta % 16 == 0))
    for h in range(H):
        slope = np.float32(2.0 ** (-8.0 * (h + 1) / H))
        c[:, C_BIAS + h * SEQ:C_BIAS + (h + 1) * SEQ] = np.where(mult > 0, -slope * delta, NEG)
    c[:, C_MULT:C_MULT + SEQ] = mult
    c[:, C_STRICT:C_STRICT + P] = row < col
    c[:, C_NEG:C_NEG + P] = np.where(row < col, 0.0, NEG)
    c[:, C_TRIL:C_TRIL + P] = row <= col
    c[:, C_IOTA:C_IOTA + TOPK] = np.arange(TOPK)
    c[:, C_EPS] = EPS
    return c


def gather_plan():
    plan = []
    for J in range(HEADS + 1):
        for k in range(TOPK):
            if J < HEADS:
                plan.append(("u", J, k))
            if J >= 1:
                plan.append(("v", J - 1, k))
    return plan


def trunk(nc, x_in, cst_in, w_in, w_out, w_q, subkeys, w_sgu, b_sgu, conv_w, g_mix, g_head, g_ffn,
          g_sgu, g_qd, g_kd, g_qs, g_ks, *rest):
    tables_u, tables_v, out = rest[:DEPTH], rest[DEPTH:2 * DEPTH], rest[2 * DEPTH]
    plan = gather_plan()
    at = {g: q for q, g in enumerate(plan)}

    with ExitStack() as ctx:
        def sb(name, shape, dt=F32):
            return ctx.enter_context(nc.sbuf_tensor(name, shape, dt))

        def ps(name, shape):
            return ctx.enter_context(nc.psum_tensor(name, shape, F32))

        def sem(name):
            return ctx.enter_context(nc.semaphore(name))

        x = sb("x", [P, NC, D])
        ring = sb("ring", [P, NB, D])
        wr = sb("wr", [P, NW, KD, PW])
        cst = sb("cst", [P, C_WIDTH])
        gains = sb("gains", [P, 3, D])
        g64 = sb("g64", [P, 4, HD])
        gsv = sb("gsv", [P, MW])
        sgw = sb("sgw", [P, H, P])
        sgb = sb("sgb", [P, H])
        cvw = sb("cvw", [P, 2, 3])
        sub = sb("sub", [P, 2 * PH, P])
        hn = sb("hn", [P, D])
        hT = sb("hT", [P, KD, P])
        htok = sb("htok", [P, 2, D])
        tm = sb("tm", [P, 6, MW])
        fm = sb("fm", [P, 3, 2, P])
        vd = sb("vd", [P, NC, MW])
        vs = sb("vs", [P, NC, MW])
        kdT = sb("kdT", [P, 2, SEQ])
        ksT = sb("ksT", [P, 2, SEQ])
        qdT = sb("qdT", [P, 2, P])
        qsT = sb("qsT", [P, 2, P])
        sq = hn
        cat = sb("cat", [P, 4, MW])
        prob = sb("prob", [P, 2, SEQ])
        probT = sb("probT", [P, 2, SEQ])
        zs, soft = prob, probT
        later = sb("later", [P, SEQ])
        stick = sb("stick", [P, NC, SEQ])
        yc = sb("yc", [P, 2, P + 2])
        cv = sb("cv", [P, 2, P])
        ss = sb("ss", [P, 16])
        rs = sb("rs", [P, 16])
        nt = sb("nt", [P, 2, 16])
        nmax = sb("nmax", [P, H])
        den = sb("den", [P, H])
        rden = sb("rden", [P, H])
        qT = sb("qT", [P, 2, 2, P])
        sc = sb("sc", [P, 2, 2, P])
        sc2 = sb("sc2", [P, 2 * P])
        sv = sb("sv", [P, 2, TOPK])
        si = sb("si", [P, 2, TOPK], U32)
        sif = sb("sif", [P, 2, TOPK])
        cand = sb("cand", [P, TOPK, TOPK])
        top = sb("top", [P, TOPK])
        pos = sb("pos", [P, 3, TOPK], U32)
        posf = sb("posf", [P, 2, TOPK])
        hot = sb("hot", [P, TOPK, TOPK])
        pick = sb("pick", [P, 2, TOPK])
        idx = sb("idx", [P, 2, SLOTS], I32)
        gate = sb("gate", [P, 2, SLOTS])
        gsum = sb("gsum", [P, PH])
        adot = sb("adot", [P, SLOTS])
        gl = sb("gl", [P, TOPK])
        gle = sb("gle", [P, TOPK])
        wgt = sb("wgt", [P, 2, TOPK])
        diag = sb("diag", [P, ND, P])

        psY = ps("psY", [P, D])
        psP = ps("psP", [P, 2, 512])
        psT = ps("psT", [P, 2, 512])
        psS = ps("psS", [P, 512])
        psO = ps("psO", [P, 512])

        ident = cst[:, C_ID:C_ID + P]
        one = cst[:, C_ONE:C_ONE + 1]
        eps = cst[:, C_EPS:C_EPS + 1]

        s_cst = sem("s_cst")
        s_x = [sem(f"s_x{c}") for c in range(NC)]
        s_par = sem("params_loaded")
        w_landed = [sem(f"w_landed{i}") for i in range(NW)]
        g_landed = [sem(f"g_landed{i}") for i in range(NB)]
        piece_used = sem("piece_used")
        piece_ready = sem("piece_ready")
        psp_act = sem("psp_act")
        psp_dve = sem("psp_dve")
        tp_ready = sem("tp_ready")
        tp_taken = sem("tp_taken")
        sumsq = sem("sumsq")
        rough = sem("rough")
        normed = sem("normed")
        qk_done = sem("qk_done")
        scored = sem("scored")
        biased = sem("biased")
        expd = sem("expd")
        weighed = sem("weighed")
        dil_out = sem("dil_out")
        z_half = sem("z_half")
        z_ready = sem("z_ready")
        z_taken = sem("z_taken")
        softed = sem("softed")
        sum_ready = sem("sum_ready")
        lesser = sem("lesser")
        sticked = sem("sticked")
        sb_out = sem("sb_out")
        pso_free = sem("pso_free")
        gelu_in = sem("gelu_in")
        gelu_e = sem("gelu_e")
        sgu_in = sem("sgu_in")
        sgu_out = sem("sgu_out")
        conv_done = sem("conv_done")
        cat_sq = sem("cat_sq")
        x_mixed = sem("x_mixed")
        s_scores = sem("s_scores")
        s_taken = sem("s_taken")
        top_exp = sem("top_exp")
        idx_ready = sem("idx_ready")
        gate_ready = sem("gate_ready")
        qk_squared = sem("qk_squared")
        v_squared = sem("v_squared")
        cat_squared = sem("cat_squared")
        gelu_done = sem("gelu_done")
        dotted = sem("dotted")
        a_exp_in = sem("a_exp_in")
        a_exp = sem("a_exp")
        w_ready = sem("w_ready")
        diag_ready = sem("diag_ready")
        v_used = sem("v_used")
        vx_used = sem("vx_used")
        x_done = sem("x_done")
        s_out = sem("s_out")
        dve_chain, act_chain = sem("dve_chain"), sem("act_chain")

        def uses_before(s):
            return sum(t % NC + 1 for t in range(s))

        def pso_use(s, n):
            return uses_before(s) + 3 * s + n

        def psp_freed(G):
            s, i = divmod(G, PIECES)
            d = N_OUT * s + min(max(i + 1 - N_IN, 0), N_OUT)
            if N_IN <= i < N_IN + N_OUT:
                return psp_dve, d
            return psp_act, (PIECES - N_OUT) * s + (i + 1 if i < N_IN else i + 1 - N_OUT)

        block = ctx.enter_context(nc.Block())

        @block.sync
        def _(sp):
            sp.dma_start(cst[:], cst_in).then_inc(s_cst, 16)
            for c in range(NC):
                sp.dma_start(x[:, c], x_in[c * P:(c + 1) * P]).then_inc(s_x[c], 16)
            for s in range(STEPS):
                l, c = divmod(s, NC)
                if c == 0:
                    if l:
                        sp.wait_ge(idx_ready, PH * s)
                    for i, g in enumerate((g_mix, g_head, g_ffn)):
                        sp.dma_start(gains[:, i], g[l].partition_broadcast(P)).then_inc(s_par, 16)
                    for i, g in enumerate((g_qd, g_kd, g_qs, g_ks)):
                        sp.dma_start(g64[:, i], g[l].partition_broadcast(P)).then_inc(s_par, 16)
                    sp.dma_start(gsv[:], g_sgu[l].partition_broadcast(P)).then_inc(s_par, 16)
                    for t, src in ((sgw, w_sgu), (sgb, b_sgu), (cvw, conv_w), (sub, subkeys)):
                        sp.dma_start(t[:], src[l]).then_inc(s_par, 16)
                for i in range(PIECES):
                    G = PIECES * s + i
                    if G >= NW:
                        sp.wait_ge(piece_used, G - NW + 1)
                    src = w_in[l, i] if i < N_IN else w_out[l, i - N_IN] if i < N_IN + N_OUT else w_q[l, i - N_IN - N_OUT]
                    sp.dma_start(wr[:, G % NW], src).then_inc(w_landed[G % NW], 16)
            for c in range(NC):
                sp.wait_ge(x_done, STEPS - NC + c + 1)
                sp.dma_start(out[c * P:(c + 1) * P], x[:, c]).then_inc(s_out, 16)
            sp.wait_ge(s_out, 16 * NC)

        N_PAR = 12 * 16

        @block.gpsimd
        def _(pool):
            for q, (kind, J, k) in enumerate(plan):
                s, h = divmod(J, PH)
                if kind == "u" and k == 0:
                    pool.wait_ge(idx_ready, J + 1)
                if q >= NB:
                    k0, J0, i0 = plan[q - NB]
                    if k0 == "u":
                        pool.wait_ge(dotted, TOPK * J0 + i0 + 1)
                    elif i0 in DVE_K:
                        pool.wait_ge(vx_used, len(DVE_K) * J0 + DVE_K.index(i0) + 1)
                    else:
                        pool.wait_ge(v_used, len(PE_K) * J0 + PE_K.index(i0) + 1)
                table = (tables_u if kind == "u" else tables_v)[s // NC]
                n = h * TOPK + k
                pool.indirect_dma_start(out=ring[:, q % NB], out_offset=None, in_=table,
                                        in_offset=bass.IndirectOffsetOnAxis(ap=idx[:, s % 2, n:n + 1], axis=0)
                                        ).then_inc(g_landed[q % NB], 16)

        def landed(eng, g):
            q = at[g]
            eng.wait_ge(g_landed[q % NB], 16 * (q // NB + 1))

        @block.scalar
        def _(act):
            made = [0]

            def link(ins):
                made[0] += 1
                ins.then_inc(act_chain, 1)
                act.wait_ge(act_chain, made[0])

            def rough_rsqrt(n, width, terms):
                act.wait_ge(sumsq, n)
                if n >= 2:
                    act.wait_ge(rough, n - 1)
                link(nc.scalar.activation(rs[:, :width], ss[:, :width], ACT.Ln, bias=eps, scale=1.0 / terms))
                nc.scalar.activation(rs[:, :width], rs[:, :width], ACT.Exp, scale=-0.5).then_inc(rough, 1)

            def take_batch(b, dst, width=512):
                act.wait_ge(tp_ready, b + 1)
                nc.scalar.activation(dst, psT[:, b % 2, :width], ACT.Copy).then_inc(tp_taken, 1)

            def row_sumsq(s):
                l, c = divmod(s, NC)
                link(nc.scalar.activation(sq[:], x[:, c], ACT.Square, accum_out=ss[:, 0:1]))
                act.sem_inc(sumsq, 1)

            def take_hT(b, count):
                if b:
                    act.wait_ge(piece_used, count)
                for i in range(2):
                    take_batch(b + i, hT[:, 4 * i:4 * i + 4].rearrange("p a b -> p (a b)"))

            def front(s, part, i):
                l, c = divmod(s, NC)
                n = 5 * s
                B = BATCHES * s
                if part == "norm1":
                    act.wait_ge(s_cst, 16)
                    act.wait_ge(s_x[c], 16)
                    if l:
                        act.wait_ge(x_done, s - NC + 1)
                    if s:
                        act.wait_ge(normed, 3 * s)
                        act.wait_ge(tp_ready, B)
                    row_sumsq(s)
                    rough_rsqrt(n + 1, 1, D)
                elif part == "hT1":
                    take_hT(B, PIECES * s)
                elif part == "piece":
                    G = PIECES * s + i
                    act.wait_ge(piece_ready, G + 1)
                    if i == 0 and s:
                        act.wait_ge(cat_sq, s)
                    if i < 4:
                        dst = tm[:, i]
                    elif i in (DV, BV):
                        dst = (vd if i == DV else vs)[:, c]
                        if l:
                            act.wait_ge(sb_out, s)
                    elif i in (SU, SV):
                        dst = tm[:, 4 + i - SU]
                    else:
                        dst = fm[:, i - CB].rearrange("p a b -> p (a b)")
                    nc.scalar.activation(dst, psP[:, G % 2, :PW], ACT.Copy).then_inc(psp_act, 1)
                elif part == "qk squares":
                    act.wait_ge(tp_ready, B + 2)
                    act.wait_ge(psp_act, (PIECES - N_OUT) * s + 4)
                    nc.scalar.activation(sq[:], tm[:, 0:4].rearrange("p a b -> p (a b)"), ACT.Square).then_inc(qk_squared, 1)
                elif part == "qk root":
                    rough_rsqrt(n + 2, 16, HD)
                elif part == "qk taken":
                    for j, (dq, dk) in enumerate(((qdT, kdT), (qsT, ksT))):
                        act.wait_ge(tp_ready, B + 2 + j + 1)
                        v = psT[:, (B + 2 + j) % 2].rearrange("p (a b) -> p a b", a=4)
                        nc.scalar.activation(dq[:], v[:, 0:2], ACT.Copy)
                        nc.scalar.activation(dk[:, :, c * P:(c + 1) * P], v[:, 2:4], ACT.Copy).then_inc(tp_taken, 1)
                elif part == "gelu exp":
                    act.wait_ge(gelu_in, s + 1)
                    nc.scalar.activation(sq[:, :2 * MW], sq[:, :2 * MW], ACT.Exp).then_inc(gelu_e, 1)
                elif part == "v squares":
                    act.wait_ge(gelu_done, s + 1)
                    nc.scalar.activation(sq[:, :MW], tm[:, 5], ACT.Square).then_inc(v_squared, 1)
                elif part == "v root":
                    rough_rsqrt(n + 3, 4, HD)
                elif part == "dil exp":
                    w = (c + 1) * P
                    act.wait_ge(biased, H * s + i + 1)
                    nc.scalar.activation(prob[:, i % 2, :w], prob[:, i % 2, :w], ACT.Exp,
                                         bias=nmax[:, i:i + 1]).then_inc(expd, 1)
                elif part == "dil taken":
                    w = (c + 1) * P
                    if i >= 2:
                        act.wait_ge(dil_out, H * s + i - 1)
                    elif s:
                        act.wait_ge(sticked, uses_before(s))
                        act.wait_ge(sum_ready, uses_before(s))
                    take_batch(B + 4 + i, probT[:, i % 2, :w], w)
                elif part == "logits":
                    if i > c:
                        return
                    u = uses_before(s) + i
                    act.wait_ge(z_ready, u + 1)
                    if i == 0:
                        act.wait_ge(dil_out, H * (s + 1))
                    if i >= 2:
                        act.wait_ge(sticked, u - 1)
                        act.wait_ge(softed, u)
                        act.wait_ge(sum_ready, u - 1)
                    link(nc.scalar.activation(soft[:, u % 2], psS[:], ACT.Abs))
                    nc.scalar.activation(zs[:, u % 2], psS[:], ACT.Copy)
                    link(nc.scalar.activation(soft[:, u % 2], soft[:, u % 2], ACT.Exp, scale=-1.0))
                    nc.scalar.activation(soft[:, u % 2], soft[:, u % 2], ACT.Ln, bias=one).then_inc(z_taken, 1)
                elif part == "stick exp":
                    if i > c:
                        return
                    u = uses_before(s) + i
                    act.wait_ge(lesser, u + 1)
                    if s:
                        act.wait_ge(sb_out, s)
                    nc.scalar.activation(stick[:, c - i], zs[:, u % 2], ACT.Exp).then_inc(sticked, 1)
                elif part == "conv taken":
                    take_batch(B + 8, cat[:, 2], MW)
                elif part == "cat squares":
                    act.wait_ge(cat_sq, s + 1)
                    nc.scalar.activation(sq[:], cat[:].rearrange("p a b -> p (a b)"), ACT.Square).then_inc(cat_squared, 1)
                elif part == "cat root":
                    rough_rsqrt(n + 4, 16, HD)
                elif part == "catT":
                    take_hT(B + 9, PIECES * s + N_IN)
                elif part == "norm2":
                    act.wait_ge(tp_ready, B + 11)
                    act.wait_ge(x_mixed, s + 1)
                    row_sumsq(s)
                    rough_rsqrt(n + 5, 1, D)
                elif part == "hT2":
                    take_hT(B + 11, PIECES * s + N_IN + N_OUT)
                elif part == "queries":
                    T, G = PH * s + i, PIECES * s + N_IN + N_OUT + i
                    act.wait_ge(piece_ready, G + 1)
                    if T >= 2:
                        act.wait_ge(s_scores, T - 1)
                    nc.scalar.activation(qT[:, T % 2].rearrange("p a b -> p (a b)"), psP[:, G % 2, :PW],
                                         ACT.Copy).then_inc(psp_act, 1)
                elif part == "key scores":
                    T = PH * s + i
                    if T >= 2:
                        act.wait_ge(idx_ready, T - 1)
                    act.wait_ge(s_scores, T + 1)
                    nc.scalar.activation(sc[:, T % 2].rearrange("p a b -> p (a b)"), psS[:, :2 * P],
                                         ACT.Copy).then_inc(s_taken, 1)
                elif part == "gate exp":
                    act.wait_ge(idx_ready, PH * (s + 1))
                    nc.scalar.activation(gate[:, s % 2], gate[:, s % 2], ACT.Exp).then_inc(top_exp, 1)

            for slot in range(SLOTS):
                for part, i in at_slot(ACT_PARTS, slot):
                    front(0, part, i)
            for J in range(HEADS + 1):
                for k in range(TOPK):
                    if J >= 1 and k in PE_K:
                        m = len(PE_K) * (J - 1) + PE_K.index(k)
                        if k == 0:
                            act.wait_ge(w_ready, J)
                        if m >= ND:
                            act.wait_ge(v_used, m - ND + 1)
                        nc.scalar.activation(diag[:, m % ND], ident, ACT.Copy,
                                             scale=wgt[:, (J - 1) % 2, k:k + 1]).then_inc(diag_ready, 1)
                    slot = J % PH * TOPK + k
                    if J + PH < HEADS:
                        for part, i in at_slot(ACT_PARTS, slot):
                            front(J // PH + 1, part, i)
                if J < HEADS:
                    act.wait_ge(a_exp_in, J + 1)
                    nc.scalar.activation(gle[:], gle[:], ACT.Exp).then_inc(a_exp, 1)

        @block.tensor
        def _(pe):
            def transposes(b, srcs):
                if b >= 2:
                    pe.wait_ge(tp_taken, b - 1)
                for i, src in enumerate(srcs):
                    last = nc.tensor.transpose(psT[:, b % 2, i * P:(i + 1) * P], src, ident)
                last.then_inc(tp_ready, 1)

            def project(s, i):
                G = PIECES * s + i
                pe.wait_ge(w_landed[G % NW], 16 * (G // NW + 1))
                if G >= 2:
                    pe.wait_ge(*psp_freed(G - 2))
                w = wr[:, G % NW]
                if CB <= i < N_IN or i >= N_IN + N_OUT:
                    for b in range(2):
                        for k in range(KD):
                            last = nc.tensor.matmul(psP[:, G % 2, b * P:(b + 1) * P], w[:, k, b * P:(b + 1) * P],
                                                    hT[:, k], start=(k == 0), stop=(k == KD - 1))
                else:
                    for k in range(KD):
                        last = nc.tensor.matmul(psP[:, G % 2, :PW], hT[:, k], w[:, k], start=(k == 0), stop=(k == KD - 1))
                last.then_inc(piece_ready, 1)
                pe.wait_ge(piece_ready, G + 1)
                pe.sem_inc(piece_used, 1)

            def score(s, h):
                l, c = divmod(s, NC)
                if h == 0:
                    pe.wait_ge(tp_taken, BATCHES * s + 4)
                    if s:
                        pe.wait_ge(s_taken, PH * s)
                else:
                    pe.wait_ge(biased, H * s + h)
                r = slice(HD * (h % 2), HD * (h % 2) + HD)
                nc.tensor.matmul(psS[:, :(c + 1) * P], qdT[r, h // 2], kdT[r, h // 2, :(c + 1) * P],
                                 start=True, stop=True).then_inc(scored, 1)

            def logits(s, i):
                l, c = divmod(s, NC)
                u = uses_before(s) + i
                if i == 0:
                    pe.wait_ge(biased, H * (s + 1))
                else:
                    pe.wait_ge(z_taken, u)
                kc = c - i
                for h in (0, 2, 1, 3):
                    if h == 1:
                        last.then_inc(z_half, 1)
                        pe.wait_ge(z_half, u + 1)
                    r = slice(HD * (h % 2), HD * (h % 2) + HD)
                    last = nc.tensor.matmul(psS[:, h * P:(h + 1) * P], ksT[r, h // 2, kc * P:(kc + 1) * P],
                                            qsT[r, h // 2], start=True, stop=True)
                last.then_inc(z_ready, 1)

            def pso_wait(s, n):
                if pso_use(s, n):
                    pe.wait_ge(pso_free, pso_use(s, n))

            def front(s, part, i):
                l, c = divmod(s, NC)
                B = BATCHES * s
                if part in ("hT1", "catT", "hT2"):
                    n, b = {"hT1": (1, 0), "catT": (2, 9), "hT2": (3, 11)}[part]
                    pe.wait_ge(normed, 3 * s + n)
                    for i in range(2):
                        transposes(B + b + i, [hn[:, (4 * i + j) * P:(4 * i + j + 1) * P] for j in range(4)])
                elif part == "piece":
                    if i in (0, N_IN, N_IN + N_OUT):
                        b = {0: 0, N_IN: 9, N_IN + N_OUT: 11}[i]
                        pe.wait_ge(tp_taken, B + b + 2)
                    project(s, i)
                elif part == "qk":
                    pe.wait_ge(qk_done, s + 1)
                    for i in range(2):
                        transposes(B + 2 + i, [hn[:, (4 * i + j) * P:(4 * i + j + 1) * P] for j in range(4)])
                elif part == "scores":
                    score(s, i)
                elif part == "dil T":
                    pe.wait_ge(weighed, H * s + i + 1)
                    transposes(B + 4 + i, [prob[:, i % 2, j * P:(j + 1) * P] for j in range(c + 1)])
                elif part == "dil out":
                    pe.wait_ge(tp_taken, B + 4 + i + 1)
                    if i == 0:
                        pso_wait(s, 0)
                        if l or c:
                            pe.wait_ge(psp_act, (PIECES - N_OUT) * s + DV + 1)
                    for j in range(c + 1):
                        last = nc.tensor.matmul(psO[:, i * HD:(i + 1) * HD], probT[:, i % 2, j * P:(j + 1) * P],
                                                vd[:, j, i * HD:(i + 1) * HD], start=(j == 0), stop=(j == c))
                    last.then_inc(dil_out, 1)
                elif part == "logits":
                    if i <= c:
                        logits(s, i)
                elif part == "sums":
                    if i > c:
                        return
                    u = uses_before(s) + i
                    pe.wait_ge(softed, u + 1)
                    pso_wait(s, 2 + i)
                    last = nc.tensor.matmul(psO[:], cst[:, C_TRI:C_TRI + P], soft[:, u % 2], start=True, stop=(i == 0))
                    if i:
                        last = nc.tensor.matmul(psO[:], cst[:, C_ONE:C_ONE + P], later[:], start=False, stop=True)
                    last.then_inc(sum_ready, 1)
                elif part == "stick out":
                    pe.wait_ge(sticked, uses_before(s + 1))
                    pso_wait(s, c + 3)
                    for h in range(H):
                        for j in range(c + 1):
                            last = nc.tensor.matmul(psO[:, h * HD:(h + 1) * HD], stick[:, j, h * P:(h + 1) * P],
                                                    vs[:, j, h * HD:(h + 1) * HD], start=(j == 0), stop=(j == c))
                    last.then_inc(sb_out, 1)
                elif part == "sgu":
                    pe.wait_ge(sgu_in, s + 1)
                    pso_wait(s, 1)
                    for h in range(H):
                        last = nc.tensor.matmul(psO[:, h * HD:(h + 1) * HD], sgw[:, h], tm[:, 5, h * HD:(h + 1) * HD],
                                                start=True, stop=True)
                    last.then_inc(sgu_out, 1)
                elif part == "conv":
                    pe.wait_ge(conv_done, s + 1)
                    transposes(B + 8, [cv[:, 0], cv[:, 1]])
                elif part == "key scores":
                    T = PH * s + i
                    pe.wait_ge(*psp_freed(PIECES * s + N_IN + N_OUT + i))
                    if i == 0:
                        pe.wait_ge(z_taken, uses_before(s + 1))
                    else:
                        pe.wait_ge(s_taken, T)
                    for b in range(2):
                        last = nc.tensor.matmul(psS[:, b * P:(b + 1) * P], qT[:, T % 2, b], sub[:, 2 * i + b],
                                                start=True, stop=True)
                    last.then_inc(s_scores, 1)

            pe.wait_ge(s_cst, 16)
            pe.wait_ge(s_par, N_PAR)
            for slot in range(SLOTS):
                for part, i in at_slot(PE_PARTS, slot):
                    front(0, part, i)
            for J in range(HEADS + 1):
                for k in range(TOPK):
                    if J >= 1 and k in PE_K:
                        s, h = divmod(J - 1, PH)
                        n = h * TOPK + k
                        m = len(PE_K) * (J - 1) + PE_K.index(k)
                        landed(pe, ("v", J - 1, k))
                        pe.wait_ge(diag_ready, m + 1)
                        if n == 0 and s:
                            pe.wait_ge(x_done, s)
                        r = ring[:, at[("v", J - 1, k)] % NB]
                        for b in range(2):
                            last = nc.tensor.matmul(psY[:, b * 512:(b + 1) * 512], diag[:, m % ND],
                                                    r[:, b * 512:(b + 1) * 512], start=(n == 0), stop=(h == PH - 1 and k == PE_K[-1]))
                        last.then_inc(v_used, 1)
                    slot = J % PH * TOPK + k
                    if J + PH < HEADS:
                        if slot == 0 and (J // PH + 1) % NC == 0:
                            pe.wait_ge(s_par, N_PAR * ((J // PH + 1) // NC + 1))
                        for part, i in at_slot(PE_PARTS, slot):
                            front(J // PH + 1, part, i)

        @block.vector
        def _(dve):
            v = nc.vector
            made = [0]

            def link(ins):
                made[0] += 1
                ins.then_inc(dve_chain, 1)
                dve.wait_ge(dve_chain, made[0])

            def sharpen(n, width, terms):
                m, r, t, u = ss[:, :width], rs[:, :width], nt[:, 0, :width], nt[:, 1, :width]
                link(v.tensor_scalar(t, m, 1.0 / terms, EPS, ALU.mult, ALU.add))
                dve.wait_ge(rough, n)
                link(v.tensor_tensor(u, r, r, ALU.mult))
                link(v.tensor_tensor(u, u, t, ALU.mult))
                link(v.tensor_scalar(u, u, -0.5, 1.5, ALU.mult, ALU.add))
                link(v.tensor_tensor(r, r, u, ALU.mult))

            def gelu_exponent(tmp, src):
                link(v.tensor_tensor(tmp, src, src, ALU.mult))
                link(v.tensor_scalar(tmp, tmp, -GELU_C * GELU_A, -GELU_C, ALU.mult, ALU.add))
                link(v.tensor_tensor(tmp, tmp, src, ALU.mult))

            def per_head(t, heads):
                return t[:, :heads].unsqueeze(2).broadcast_to([P, heads, HD])

            def top16(src, values, places, width):
                link(v.max(values[:, 0:8], src))
                link(v.max_index(places[:, 0:8], values[:, 0:8], src))
                link(v.match_replace(sc2[:, :width], values[:, 0:8], src, LOWEST))
                link(v.max(values[:, 8:16], sc2[:, :width]))
                link(v.max_index(places[:, 8:16], values[:, 8:16], sc2[:, :width]))

            def across_heads(o):
                return cst[:, o:o + P].unsqueeze(1).broadcast_to([P, H, P])

            def front(s, part, i):
                l, c = divmod(s, NC)
                n = 5 * s
                if part == "norm1":
                    dve.wait_ge(sumsq, n + 1)
                    sharpen(n + 1, 1, D)
                    v.scalar_tensor_tensor(out=hn[:], in0=x[:, c], scalar=rs[:, 0:1], in1=gains[:, 0],
                                           op0=ALU.mult, op1=ALU.mult).then_inc(normed, 1)
                elif part == "qk sums":
                    dve.wait_ge(qk_squared, s + 1)
                    v.tensor_reduce(ss[:], sq[:].rearrange("p (h d) -> p h d", d=HD), AX.X, ALU.add).then_inc(sumsq, 1)
                elif part == "qk":
                    dve.wait_ge(sumsq, n + 2)
                    sharpen(n + 2, 16, HD)
                    hv = hn[:].rearrange("p (h d) -> p h d", d=HD)
                    link(v.tensor_tensor(hv, tm[:, 0:4].rearrange("p a (h d) -> p (a h) d", d=HD), per_head(rs, 16), ALU.mult))
                    h4 = hn[:].rearrange("p (a h d) -> p a h d", a=4, d=HD)
                    link(v.tensor_tensor(h4, h4, g64[:].unsqueeze(2).broadcast_to([P, 4, H, HD]), ALU.mult))
                    q = hn[:].rearrange("p (a b c) -> p a b c", a=2, b=2)[:, :, 0]
                    v.tensor_scalar(q, q, HD ** -0.5, None, ALU.mult).then_inc(qk_done, 1)
                elif part == "bias":
                    w, N = (c + 1) * P, H * s + i
                    pr = prob[:, i % 2, :w]
                    o = C_BIAS + i * SEQ + (NC - 1 - c) * P
                    if i == 0 and s:
                        dve.wait_ge(sticked, uses_before(s))
                    if i >= 2:
                        dve.wait_ge(tp_ready, BATCHES * s + 4 + i - 1)
                    dve.wait_ge(scored, N + 1)
                    link(v.tensor_tensor(pr, psS[:, :w], cst[:, o:o + w], ALU.add))
                    v.tensor_reduce(nmax[:, i:i + 1], pr, AX.X, ALU.max, negate=True).then_inc(biased, 1)
                elif part == "weigh":
                    w, N = (c + 1) * P, H * s + i
                    pr = prob[:, i % 2, :w]
                    dve.wait_ge(expd, N + 1)
                    o = C_MULT + (NC - 1 - c) * P
                    v.tensor_tensor_reduce(out=pr, in0=pr, in1=cst[:, o:o + w], scale=1.0, scalar=0.0, op0=ALU.mult,
                                           op1=ALU.add, accum_out=den[:, i:i + 1]).then_inc(weighed, 1)
                elif part == "dil out":
                    dve.wait_ge(weighed, H * (s + 1))
                    link(v.reciprocal(rden[:], den[:]))
                    dve.wait_ge(dil_out, H * (s + 1))
                    if s:
                        dve.wait_ge(cat_squared, s)
                    v.tensor_tensor(cat[:, 1].rearrange("p (h d) -> p h d", d=HD),
                                    psO[:, :MW].rearrange("p (h d) -> p h d", d=HD), per_head(rden, H),
                                    ALU.mult).then_inc(pso_free, 1)
                elif part == "softplus":
                    if i > c:
                        return
                    u = uses_before(s) + i
                    z, f = zs[:, u % 2], soft[:, u % 2]
                    dve.wait_ge(z_taken, u + 1)
                    if i == 1:
                        if s:
                            dve.wait_ge(sum_ready, u)
                        link(v.tensor_copy(later[:], soft[:, (u - 1) % 2]))
                    elif i > 1:
                        dve.wait_ge(sum_ready, u)
                        link(v.tensor_tensor(later[:], later[:], soft[:, (u - 1) % 2], ALU.add))
                    ins = v.scalar_tensor_tensor(out=f, in0=z, scalar=0.0, in1=f, op0=ALU.max, op1=ALU.add)
                    if i == 0:
                        link(ins)
                        fm4 = f.rearrange("p (h q) -> p h q", q=P)
                        ins = v.tensor_tensor(fm4, fm4, across_heads(C_STRICT), ALU.mult)
                    ins.then_inc(softed, 1)
                elif part == "exponent":
                    if i > c:
                        return
                    u = uses_before(s) + i
                    z = zs[:, u % 2]
                    dve.wait_ge(sum_ready, u + 1)
                    v.tensor_tensor(z, z, psO[:], ALU.subtract).then_inc(pso_free, 1)
                    dve.wait_ge(pso_free, pso_use(s, 3 + i))
                    if i == 0:
                        link(v.tensor_scalar(z, z, 0.0, None, ALU.min))
                        z4 = z.rearrange("p (h q) -> p h q", q=P)
                        v.tensor_tensor(z4, z4, across_heads(C_NEG), ALU.add).then_inc(lesser, 1)
                    else:
                        v.tensor_scalar(z, z, 0.0, None, ALU.min).then_inc(lesser, 1)
                elif part == "stick out":
                    dve.wait_ge(sb_out, s + 1)
                    v.tensor_copy(cat[:, 3], psO[:, :MW]).then_inc(pso_free, 1)
                elif part == "gelu in":
                    dve.wait_ge(tp_ready, BATCHES * s + 4)
                    dve.wait_ge(psp_act, (PIECES - N_OUT) * s + SV + 1)
                    e = sq[:, :2 * MW]
                    gelu_exponent(e, tm[:, 4:6].rearrange("p a b -> p (a b)"))
                    v.tensor_scalar(e, e, EXP_CAP, None, ALU.min).then_inc(gelu_in, 1)
                elif part == "gelu":
                    e, uv = sq[:, :2 * MW], tm[:, 4:6].rearrange("p a b -> p (a b)")
                    dve.wait_ge(gelu_e, s + 1)
                    link(v.tensor_scalar(e, e, 1.0, None, ALU.add))
                    link(v.reciprocal(e, e))
                    v.tensor_tensor(uv, uv, e, ALU.mult).then_inc(gelu_done, 1)
                    if c == 0:
                        if l:
                            dve.wait_ge(sgu_out, s)
                        link(v.tensor_tensor(sgw[:], sgw[:], across_heads(C_TRIL), ALU.mult))
                elif part == "v sums":
                    dve.wait_ge(v_squared, s + 1)
                    v.tensor_reduce(ss[:, :H], sq[:, :MW].rearrange("p (h d) -> p h d", d=HD), AX.X, ALU.add).then_inc(sumsq, 1)
                elif part == "sgu in":
                    dve.wait_ge(sumsq, n + 3)
                    sharpen(n + 3, H, HD)
                    vv = tm[:, 5].rearrange("p (h d) -> p h d", d=HD)
                    link(v.tensor_tensor(vv, vv, per_head(rs, H), ALU.mult))
                    v.tensor_tensor(tm[:, 5], tm[:, 5], gsv[:], ALU.mult).then_inc(sgu_in, 1)
                elif part == "sgu":
                    dve.wait_ge(sgu_out, s + 1)
                    for h in range(H):
                        o = slice(h * HD, (h + 1) * HD)
                        last = v.scalar_tensor_tensor(out=cat[:, 0, o], in0=psO[:, o], scalar=sgb[:, h:h + 1],
                                                      in1=tm[:, 4, o], op0=ALU.add, op1=ALU.mult)
                    last.then_inc(pso_free, 1)
                elif part == "conv":
                    dve.wait_ge(psp_act, (PIECES - N_OUT) * s + N_IN)
                    if c == 0:
                        link(v.memset(yc[:, :, 0:2], 0.0))
                    else:
                        link(v.tensor_copy(yc[:, :, 0:2], yc[:, :, P:P + 2]))
                    link(v.tensor_tensor(yc[:, :, 2:], fm[:, 1], fm[:, 2], ALU.mult))
                    if s:
                        dve.wait_ge(tp_ready, BATCHES * (s - 1) + 9)
                    for b in range(2):
                        link(v.tensor_scalar(cv[:, b], yc[:, b, 0:P], cvw[:, b, 0:1], None, ALU.mult))
                        for t in (1, 2):
                            link(v.scalar_tensor_tensor(out=cv[:, b], in0=yc[:, b, t:t + P], scalar=cvw[:, b, t:t + 1],
                                                        in1=cv[:, b], op0=ALU.mult, op1=ALU.add))
                    v.tensor_tensor(cv[:], cv[:], fm[:, 0], ALU.mult).then_inc(conv_done, 1)
                elif part == "cat sums":
                    dve.wait_ge(cat_squared, s + 1)
                    v.tensor_reduce(ss[:], sq[:].rearrange("p (h d) -> p h d", d=HD), AX.X, ALU.add).then_inc(sumsq, 1)
                elif part == "cat":
                    dve.wait_ge(sumsq, n + 4)
                    sharpen(n + 4, 16, HD)
                    hv = hn[:].rearrange("p (h d) -> p h d", d=HD)
                    link(v.tensor_tensor(hv, cat[:].rearrange("p a (h d) -> p (a h) d", d=HD), per_head(rs, 16), ALU.mult))
                    v.tensor_tensor(hn[:], hn[:], gains[:, 1], ALU.mult).then_inc(normed, 1)
                elif part == "out":
                    G = PIECES * s + N_IN + i
                    dve.wait_ge(piece_ready, G + 1)
                    xs = x[:, c, i * PW:(i + 1) * PW]
                    v.tensor_tensor(xs, xs, psP[:, G % 2, :PW], ALU.add).then_inc(psp_dve, 1)
                elif part == "norm2":
                    dve.wait_ge(sumsq, n + 5)
                    sharpen(n + 5, 1, D)
                    if s >= 2:
                        dve.wait_ge(dotted, SLOTS * (s - 1))
                    link(v.scalar_tensor_tensor(out=htok[:, s % 2], in0=x[:, c], scalar=rs[:, 0:1], in1=gains[:, 2],
                                                op0=ALU.mult, op1=ALU.mult))
                    v.tensor_copy(hn[:], htok[:, s % 2]).then_inc(normed, 1)
                elif part == "top keys":
                    dve.wait_ge(s_taken, PH * s + i + 1)
                    for b in range(2):
                        top16(sc[:, (PH * s + i) % 2, b], sv[:, b], si[:, b], P)
                elif part == "top pairs":
                    if i == 0 and s >= 2:
                        dve.wait_ge(v_used, len(PE_K) * PH * (s - 1))
                        dve.wait_ge(vx_used, len(DVE_K) * PH * (s - 1))
                    o = slice(i * TOPK, (i + 1) * TOPK)
                    link(v.tensor_tensor(cand[:], sv[:, 0].unsqueeze(2).broadcast_to([P, TOPK, TOPK]),
                                         sv[:, 1].unsqueeze(1).broadcast_to([P, TOPK, TOPK]), ALU.add))
                    top16(cand[:].rearrange("p a b -> p (a b)"), top, pos[:, 0], TOPK * TOPK)
                    link(v.tensor_scalar(gate[:, s % 2, o], top[:], top[:, 0:1], None, ALU.subtract))
                    link(v.tensor_copy(sif[:], si[:]))
                    link(v.tensor_scalar(pos[:, 1], pos[:, 0], 4, None, ALU.logical_shift_right))
                    link(v.tensor_scalar(pos[:, 2], pos[:, 0], 15, None, ALU.bitwise_and))
                    link(v.tensor_copy(posf[:], pos[:, 1:3]))
                    for b in range(2):
                        link(v.tensor_tensor(hot[:], posf[:, b].unsqueeze(2).broadcast_to([P, TOPK, TOPK]),
                                             cst[:, C_IOTA:C_IOTA + TOPK].unsqueeze(1).broadcast_to([P, TOPK, TOPK]), ALU.is_equal))
                        link(v.tensor_tensor(hot[:], hot[:], sif[:, b].unsqueeze(1).broadcast_to([P, TOPK, TOPK]), ALU.mult))
                        link(v.tensor_reduce(pick[:, b], hot[:], AX.X, ALU.add))
                    v.scalar_tensor_tensor(out=idx[:, s % 2, o], in0=pick[:, 0], scalar=float(P), in1=pick[:, 1],
                                           op0=ALU.mult, op1=ALU.add).then_inc(idx_ready, 1)
                elif part == "gate":
                    dve.wait_ge(top_exp, s + 1)
                    g = gate[:, s % 2].rearrange("p (h k) -> p h k", k=TOPK)
                    link(v.tensor_reduce(gsum[:], g, AX.X, ALU.add))
                    link(v.reciprocal(gsum[:], gsum[:]))
                    v.tensor_tensor(g, g, gsum[:].unsqueeze(2).broadcast_to([P, PH, TOPK]), ALU.mult).then_inc(gate_ready, 1)

                if part == "stick out":
                    dve.wait_ge(tp_taken, BATCHES * s + 9)
                    dve.wait_ge(pso_free, pso_use(s + 1, 0))
                    dve.sem_inc(cat_sq, 1)
                if part == "out" and i == N_OUT - 1:
                    dve.wait_ge(psp_dve, N_OUT * (s + 1))
                    dve.sem_inc(x_mixed, 1)

            def add_peer(s):
                dve.wait_ge(v_used, len(PE_K) * PH * (s + 1))
                dve.wait_ge(vx_used, len(DVE_K) * PH * (s + 1))
                v.tensor_tensor(x[:, s % NC], x[:, s % NC], psY[:], ALU.add).then_inc(x_done, 1)

            dve.wait_ge(s_cst, 16)
            dve.wait_ge(s_par, N_PAR)
            for slot in range(SLOTS):
                for part, i in at_slot(DVE_PARTS, slot):
                    front(0, part, i)
            for J in range(HEADS + 1):
                s, h = divmod(J, PH)
                for k in range(TOPK):
                    if J < HEADS:
                        n = h * TOPK + k
                        landed(dve, ("u", J, k))
                        r = ring[:, at[("u", J, k)] % NB]
                        v.tensor_tensor_reduce(out=r, in0=r, in1=htok[:, s % 2], scale=1.0, scalar=0.0,
                                               op0=ALU.mult, op1=ALU.add, accum_out=adot[:, n:n + 1]).then_inc(dotted, 1)
                    if J >= 1 and k in DVE_K:
                        m = len(DVE_K) * (J - 1) + DVE_K.index(k)
                        xs = x[:, (J - 1) // PH % NC]
                        landed(dve, ("v", J - 1, k))
                        dve.wait_ge(w_ready, J)
                        if m:
                            dve.wait_ge(vx_used, m)
                        v.scalar_tensor_tensor(out=xs, in0=ring[:, at[("v", J - 1, k)] % NB],
                                               scalar=wgt[:, (J - 1) % 2, k:k + 1], in1=xs,
                                               op0=ALU.mult, op1=ALU.add).then_inc(vx_used, 1)
                    slot = h * TOPK + k
                    if J + PH < HEADS:
                        if slot == 0 and (s + 1) % NC == 0:
                            dve.wait_ge(s_par, N_PAR * ((s + 1) // NC + 1))
                        for part, i in at_slot(DVE_PARTS, slot):
                            front(s + 1, part, i)
                if J < HEADS:
                    if h == 0:
                        dve.wait_ge(gate_ready, s + 1)
                    a = adot[:, h * TOPK:(h + 1) * TOPK]
                    dve.wait_ge(dotted, TOPK * (J + 1))
                    gelu_exponent(gl[:], a)
                    v.tensor_scalar(gle[:], gl[:], EXP_CAP, None, ALU.min).then_inc(a_exp_in, 1)
                    dve.wait_ge(a_exp, J + 1)
                    link(v.tensor_scalar(gl[:], gle[:], 1.0, None, ALU.add))
                    link(v.reciprocal(gl[:], gl[:]))
                    link(v.tensor_tensor(gl[:], gl[:], a, ALU.mult))
                    if J >= 2:
                        dve.wait_ge(diag_ready, len(PE_K) * (J - 1))
                    v.tensor_tensor(wgt[:, J % 2], gl[:], gate[:, s % 2, h * TOPK:(h + 1) * TOPK], ALU.mult).then_inc(w_ready, 1)
                if J >= PH and J % PH == 0:
                    add_peer(J // PH - 1)


def kernel(x, g_mix_norm, w_in, w_sgu, b_sgu, g_sgu_v, g_q_dil, g_k_dil, conv_w, g_q_sb, g_k_sb, g_head_out,
           w_out, g_ffn_norm, w_peer_q, peer_sub_keys, peer_u, peer_v):
    import concourse.bacc as bacc
    from concourse.bass_utils import run_bass_kernel_spmd

    def pieces(w):
        w = np.asarray(w)
        return w.reshape(DEPTH, KD, P, -1, PW).transpose(0, 3, 2, 1, 4)

    ins = {
        "x": np.asarray(x).reshape(SEQ, D),
        "cst": constants(),
        "w_in": pieces(w_in)[:, IN_ORDER],
        "w_out": pieces(w_out),
        "w_q": pieces(w_peer_q),
        "subkeys": np.asarray(peer_sub_keys).reshape(DEPTH, 2 * PH, P, P).transpose(0, 3, 1, 2),
        "w_sgu": np.asarray(w_sgu).transpose(0, 3, 1, 2),
        "b_sgu": np.asarray(b_sgu).transpose(0, 2, 1),
        "conv_w": np.asarray(conv_w).reshape(DEPTH, 3, 2, P).transpose(0, 3, 2, 1),
        "g_mix": np.asarray(g_mix_norm), "g_head": np.asarray(g_head_out), "g_ffn": np.asarray(g_ffn_norm),
        "g_sgu": np.asarray(g_sgu_v), "g_qd": np.asarray(g_q_dil), "g_kd": np.asarray(g_k_dil),
        "g_qs": np.asarray(g_q_sb), "g_ks": np.asarray(g_k_sb),
        "u0": np.asarray(peer_u)[0], "u1": np.asarray(peer_u)[1],
        "v0": np.asarray(peer_v)[0], "v1": np.asarray(peer_v)[1],
    }
    nc = bacc.Bacc("TRN2", target_bir_lowering=False, num_devices=1)
    arrays, args = {}, []
    for name, a in ins.items():
        a = np.ascontiguousarray(a)
        arrays["in_" + name] = a
        args.append(nc.dram_tensor("in_" + name, a.shape, mybir.dt.from_np(a.dtype), kind="ExternalInput").ap())
    args.append(nc.dram_tensor("out", (SEQ, D), F32, kind="ExternalOutput").ap())
    trunk(nc, *args)
    r = run_bass_kernel_spmd(nc, [arrays], core_ids=[0])
    return r.results[0]["out"].reshape(1, SEQ, D)
```

```python
from contextlib import ExitStack

import numpy as np
import concourse.bass as bass
from concourse import mybir

F32 = mybir.dt.float32
U32 = mybir.dt.uint32
I32 = mybir.dt.int32
ALU = mybir.AluOpType
ACT = mybir.ActivationFunctionType
AX = mybir.AxisListType

P = 128
D = 1024
SEQ = 512
DEPTH = 2
NC = SEQ // P
STEPS = DEPTH * NC
KD = D // P
H, HD = 4, 64
MW = H * HD
PW = 256
N_IN, N_OUT, N_Q = 11, D // PW, 8
PH, TOPK = 8, 16
SLOTS = PH * TOPK
HEADS = STEPS * PH
EPS = 1e-6
NEG = -1e30
FAR = 1e33
SLOPES = [2.0 ** (-8.0 * (h + 1) / H) for h in range(H)]
LOWEST = -3.0e38
ROOT_MAGIC = 0x5F3759DF
NEWTON = 3

IN_ORDER = [2, 3, 8, 9, 4, 10, 0, 1, 5, 6, 7]
DV, BV, SU, SV, CB = 4, 5, 6, 7, 8

NB = 12
W_EARLY = 12
NW = 2
ND = 4
NS = 3

GROUPS = [((0,), -72, 1.0, 1.0), ((1,), 22, 1.0, 0.95), ((2, 3), 126, 0.7, 1.2), ((4, 5), 336, 1.15, 1.3),
          ((6, 7), 594, 0.97, 1.5)]
GROUP_OF = {s: steps for steps, *_ in GROUPS for s in steps}


def mixer_parts(s, at):
    end = 20 + 6 * (s % NC + 1)
    p = [("act", at + t, part, 0) for t, part in
         ((14.5, "v squares"), (19, "conv taken"), (end + 2, "cat squares"), (end + 5, "catT"))]
    p += [("pe", at + t, part, 0) for t, part in ((18, "conv"), (21, "sgu"), (end, "stick out"), (end + 4, "catT"))]
    p += [("dve", at + t, part, 0) for t, part in
          ((16.5, "sgu in"), (15, "conv"), (19.5, "dil out"), (22, "sgu"), (end + 1, "stick out"), (end + 3, "cat"))]
    for h in range(H):
        o = at + 4 * h
        p += [("pe", o, "scores", h), ("dve", o + 1, "bias", h), ("act", o + 2, "dil exp", h),
              ("dve", o + 3, "weigh", h), ("pe", o + 4, "dil T", h), ("act", o + 5, "dil taken", h),
              ("pe", o + 6, "dil out", h)]
    for i in range(s % NC + 1):
        o = at + 20 + 6 * i
        p += [("pe", o, "logits", i), ("act", o + 1, "logits", i), ("dve", o + 2, "softplus", i),
              ("pe", o + 3, "sums", i), ("dve", o + 4, "exponent", i), ("act", o + 5, "stick exp", i)]
    return p, at + end


def top_parts(at):
    return [("pe", at, "key scores"), ("act", at + 0.5, "key scores"), ("dve", at + 1, "top keys"),
            ("dve", at + 2, "top pairs"), ("act", at + 3, "gate exp"), ("dve", at + 4, "gate")]


def front_parts(steps):
    p, a, n = [], steps[0], len(steps)

    def add(parts, s):
        p.extend((eng, t, part, s, i) for eng, t, part, i in parts)

    for j, s in enumerate(steps):
        o = 4 * j
        add([("act", o, "norm1", 0), ("dve", o + 1, "norm1", 0), ("pe", o + 2, "hT1", 0), ("act", o + 3, "hT1", 0)], s)
    start = 4 * n
    for i in range(N_IN):
        o = start + 2 * n * i
        add([("pe", o, "piece", i), ("act", o + n, "piece", i)], a)
    for j, s in enumerate(steps):
        o = start + 8 * n + 6 * j
        add([("act", o, "qk squares", 0), ("dve", o + 1, "qk", 0), ("pe", o + 3, "qk", 0), ("act", o + 4, "qk taken", 0)], s)
    out = 18 if n == 1 else 50
    for s in steps:
        parts, out = mixer_parts(s, out)
        add(parts, s)
    out += 6
    gap = 1.5 if n == 1 else 2 * n
    for i in range(N_OUT):
        add([("pe", out + gap * i, "piece", N_IN + i), ("dve", out + gap * i + n, "out", i)], a)
    second = out + N_OUT * gap - 1
    for j, s in enumerate(steps):
        o = second + 4 * j
        add([("act", o, "norm2", 0), ("dve", o + 1, "norm2", 0), ("pe", o + 2, "hT2", 0), ("act", o + 3, "hT2", 0)], s)
    top = second + 4 * n
    for h in range(PH):
        o = top + (5 * n - n // 2) * h
        add([("pe", o, "piece", N_IN + N_OUT + h), ("act", o + n, "queries", h)], a)
        for j, s in enumerate(steps):
            p.extend((eng, t, part, s, h) for eng, t, part in top_parts(o + n + 1 + 4 * j))
    return p, top


def part_tables():
    tables = {"act": [], "pe": [], "dve": []}
    for steps, start, rate, top_rate in GROUPS:
        parts, top = front_parts(steps)
        for eng, t, part, s, i in parts:
            tables[eng].append((start + rate * min(t, top) + top_rate * max(t - top, 0), part, s, i))
    return {eng: sorted(rows, key=lambda row: row[0]) for eng, rows in tables.items()}


PARTS = part_tables()
FIRST_SLOT = int(min(row[0] for rows in PARTS.values() for row in rows)) - 1


def at_slot(eng, slot):
    return [row[1:] for row in PARTS[eng] if slot <= row[0] < slot + 1]


def numbers(eng, *names):
    rows = [row[1:] for row in PARTS[eng] if row[1] in names]
    return {row: n for n, row in enumerate(rows)}


PIECE_NO = {(s, i): n for (_, s, i), n in numbers("pe", "piece").items()}
PIECE_LIST = list(PIECE_NO)
TOP_NO = {(s, h): n for (_, s, h), n in numbers("dve", "top pairs").items()}
QUERY_NO = {(s, h): n for (_, s, h), n in numbers("act", "queries").items()}
NORM_NO = {(part, s): n for (part, s, _), n in numbers("dve", "norm1", "qk", "sgu in", "cat", "norm2").items()}
NORMED_NO = {(part, s): n for (part, s, _), n in numbers("dve", "norm1", "cat", "norm2").items()}
PSO_NO = {key: n for n, key in enumerate(
    k for k in numbers("pe", "dil out", "sgu", "sums", "stick out") if k[0] != "dil out" or k[2] == 0)}
PSS_LIST = list(numbers("pe", "scores", "logits", "key scores"))
HN_LIST = [(part, s) for part, s, _ in numbers("dve", "norm1", "qk", "sgu in", "cat", "norm2")]
BATCH_NO, _batches = {}, 0
for _part, _s, _i in numbers("pe", "hT1", "qk", "dil T", "conv", "catT", "hT2"):
    BATCH_NO[_part, _s, _i] = _batches
    _batches += 1 if _part in ("dil T", "conv") else 2


def vector_rows(J):
    return BUSY_ROWS.get(J, (3, 7, 11, 15))


BUSY_ROWS = {J: (1, 3, 5, 7, 9, 11, 13, 15) for J in range(8, 15)}
BUSY_ROWS.update({J: (7, 15) for lo, hi in ((5, 7), (15, 20), (30, 36), (46, 53)) for J in range(lo, hi)})
V_NO, _counts = {}, [0, 0]
for _J in range(HEADS):
    for _k in range(TOPK):
        _by = int(_k in vector_rows(_J))
        V_NO[_J, _k] = _by, _counts[_by]
        _counts[_by] += 1


def v_rows(J, by):
    return sum(V_NO[K, k][0] == by for K in range(J) for k in range(TOPK))


C_ID, C_TRI, C_ONE, C_DELTA = 0, P, 2 * P, 3 * P
C_MULT = C_DELTA + SEQ
C_STRICT = C_MULT + SEQ
C_NEG = C_STRICT + P
C_TRIL = C_NEG + P
C_IOTA = C_TRIL + P
C_WIDTH = C_IOTA + TOPK


def constants():
    c = np.zeros((P, C_WIDTH), np.float32)
    row, col = np.arange(P)[:, None], np.arange(P)[None, :]
    c[:, C_ID:C_ID + P] = row == col
    c[:, C_TRI:C_TRI + P] = row >= col
    c[:, C_ONE:C_ONE + P] = 1.0
    delta = row + (NC - 1) * P - np.arange(SEQ)[None, :]
    mult = ((delta >= 0) & (delta <= 128)).astype(np.float32) + ((delta >= 0) & (delta % 4 == 0)) \
        + ((delta >= 0) & (delta % 16 == 0))
    c[:, C_DELTA:C_DELTA + SEQ] = np.where(mult > 0, delta, FAR)
    c[:, C_MULT:C_MULT + SEQ] = mult
    c[:, C_STRICT:C_STRICT + P] = row < col
    c[:, C_NEG:C_NEG + P] = np.where(row < col, 0.0, NEG)
    c[:, C_TRIL:C_TRIL + P] = row <= col
    c[:, C_IOTA:C_IOTA + TOPK] = np.arange(TOPK)
    return c


def gather_plan():
    plan = []
    for J in range(HEADS + 1):
        for k in range(TOPK):
            if J < HEADS:
                plan.append(("u", J, k))
            if J >= 1:
                plan.append(("v", J - 1, k))
    return plan


def trunk(nc, x_in, cst_in, w_in, w_out, w_q, subkeys, w_sgu, b_sgu, conv_w, g_mix, g_head, g_ffn,
          g_sgu, g_qd, g_kd, g_qs, g_ks, *rest):
    tables_u, tables_v, out = rest[:DEPTH], rest[DEPTH:2 * DEPTH], rest[2 * DEPTH]
    plan = gather_plan()
    at = {g: q for q, g in enumerate(plan)}

    with ExitStack() as ctx:
        def sb(name, shape, dt=F32):
            return ctx.enter_context(nc.sbuf_tensor(name, shape, dt))

        def ps(name, shape):
            return ctx.enter_context(nc.psum_tensor(name, shape, F32))

        def sem(name):
            return ctx.enter_context(nc.semaphore(name))

        x = sb("x", [P, NC, D])
        ring = sb("ring", [P, NB, D])
        wr = sb("wr", [P, NW, KD, PW])
        cst = sb("cst", [P, C_WIDTH])
        gain_f = sb("gain_f", [P, D])
        gain_t = sb("gain_t", [P, 2, KD])
        g64 = sb("g64", [P, 4, HD])
        gsv = sb("gsv", [P, MW])
        sgw = sb("sgw", [P, H, P])
        sgb = sb("sgb", [P, H])
        cvw = sb("cvw", [P, 2, 3])
        sub = sb("sub", [P, 2 * PH, P])
        hn = sb("hn", [P, D])
        hT = sb("hT", [P, KD, 2 * P])
        htok = sb("htok", [P, NS, D])
        tm = sb("tm", [P, 2, 6, MW])
        fm = sb("fm", [P, 3, 2, 2, P])
        vd = sb("vd", [P, NC, MW])
        vs = sb("vs", [P, NC, MW])
        kdT = sb("kdT", [P, 2, SEQ])
        ksT = sb("ksT", [P, 2, SEQ])
        qdT = sb("qdT", [P, 2, 2, P])
        qsT = sb("qsT", [P, 2, 2, P])
        sq = hn
        cat = sb("cat", [P, 4, MW])
        prob = sb("prob", [P, 2, SEQ])
        probT = sb("probT", [P, 2, SEQ])
        zs, soft = prob, probT
        later = sb("later", [P, SEQ])
        stick = sb("stick", [P, NC, SEQ])
        yc = sb("yc", [P, 2, P + 2])
        cv = sb("cv", [P, 2, P])
        ss = sb("ss", [P, 16])
        rs = sb("rs", [P, 16])
        nt = sb("nt", [P, 2, 16])
        nmax = sb("nmax", [P, H])
        den = sb("den", [P, H])
        rden = sb("rden", [P, H])
        qT = sb("qT", [P, 2, 2, 2 * P])
        sc = sb("sc", [P, 2, 2, P])
        sc2 = sb("sc2", [P, 2 * P])
        sv = sb("sv", [P, 2, TOPK])
        si = sb("si", [P, 2, TOPK], U32)
        cand = sb("cand", [P, TOPK, TOPK])
        top = sb("top", [P, TOPK])
        pos = sb("pos", [P, 3, TOPK], U32)
        hot = sb("hot", [P, 2, TOPK, TOPK])
        pick = sb("pick", [P, 2, TOPK])
        idx = sb("idx", [P, NS, SLOTS], I32)
        gate = sb("gate", [P, NS, SLOTS])
        gsum = sb("gsum", [P, 1])
        rsum = sb("rsum", [P, 1])
        adot = sb("adot", [P, SLOTS])
        gl = sb("gl", [P, TOPK])
        wgt = sb("wgt", [P, 2, TOPK])
        diag = sb("diag", [P, ND, P])

        psY = ps("psY", [P, D])
        psP = ps("psP", [P, 2, 512])
        psT = ps("psT", [P, 2, 512])
        psS = ps("psS", [P, 512])
        psO = ps("psO", [P, 512])

        ident = cst[:, C_ID:C_ID + P]
        one = cst[:, C_ONE:C_ONE + 1]

        s_cst = sem("s_cst")
        s_x = [sem(f"s_x{c}") for c in range(NC)]
        s_par = sem("params_loaded")
        s_late = sem("late_params_loaded")
        w_landed = [sem(f"w_landed{i}") for i in range(NW)]
        we_landed = [sem(f"we_landed{i}") for i in range(NB // 2)]
        g_landed = [sem(f"g_landed{i}") for i in range(NB)]
        piece_ready = sem("piece_ready")
        psp_act = sem("psp_act")
        psp_dve = sem("psp_dve")
        tp_ready = sem("tp_ready")
        tp_taken = sem("tp_taken")
        sumsq = sem("sumsq")
        normed = sem("normed")
        qk_done = sem("qk_done")
        scored = sem("scored")
        biased = sem("biased")
        expd = sem("expd")
        weighed = sem("weighed")
        dil_out = sem("dil_out")
        z_half = sem("z_half")
        z_ready = sem("z_ready")
        z_taken = sem("z_taken")
        softed = sem("softed")
        sum_ready = sem("sum_ready")
        lesser = sem("lesser")
        sticked = sem("sticked")
        sb_out = sem("sb_out")
        pso_free = sem("pso_free")
        sgu_in = sem("sgu_in")
        sgu_out = sem("sgu_out")
        conv_done = sem("conv_done")
        cat_sq = sem("cat_sq")
        x_mixed = sem("x_mixed")
        s_scores = sem("s_scores")
        s_taken = sem("s_taken")
        top_exp = sem("top_exp")
        idx_ready = sem("idx_ready")
        gate_ready = sem("gate_ready")
        qk_squared = sem("qk_squared")
        v_squared = sem("v_squared")
        cat_squared = sem("cat_squared")
        dotted = sem("dotted")
        a_gelu = sem("a_gelu")
        w_ready = sem("w_ready")
        diag_ready = sem("diag_ready")
        v_used = sem("v_used")
        vx_used = sem("vx_used")
        x_done = sem("x_done")
        s_out = sem("s_out")
        dve_chain, act_chain = sem("dve_chain"), sem("act_chain")

        def uses_before(s):
            return sum(t % NC + 1 for t in range(s))

        def piece_at(G):
            if G < W_EARLY:
                n = NB // 2
                return (ring[:, 2 * (G % n):2 * (G % n) + 2].rearrange("p a (k w) -> p (a k) w", w=PW),
                        we_landed[G % n], 16 * (G // n + 1), G - n + 1)
            return wr[:, G % NW], w_landed[G % NW], 16 * ((G - W_EARLY) // NW + 1), G - NW + 1 if G >= W_EARLY + NW else 0

        def psp_sem(i):
            return psp_dve if N_IN <= i < N_IN + N_OUT else psp_act

        def psp_freed(G):
            freed = psp_sem(PIECE_LIST[G][1])
            return freed, sum(psp_sem(i) is freed for _, i in PIECE_LIST[:G + 1])

        def hn_free(part, s):
            n = HN_LIST.index((part, s))
            if n == 0:
                return None
            part, s = HN_LIST[n - 1]
            if part == "sgu in":
                return sumsq, NORM_NO["sgu in", s] + 1
            return tp_ready, BATCH_NO[{"norm1": "hT1", "qk": "qk", "cat": "catT", "norm2": "hT2"}[part], s, 0] + 2

        def pss_free(part, s, i):
            n = PSS_LIST.index((part, s, i))
            if n == 0:
                return None
            part, s, i = PSS_LIST[n - 1]
            return {"scores": (biased, H * s + i + 1), "logits": (z_taken, uses_before(s) + i + 1),
                    "key scores": (s_taken, TOP_NO.get((s, i), 0) + 1)}[part]

        def wait_for(eng, what):
            if what is not None:
                eng.wait_ge(*what)

        block = ctx.enter_context(nc.Block())

        @block.sync
        def _(sp):
            def parameters(l):
                for dst, src in ((gain_t[:, 0], g_mix), (gain_t[:, 1], g_head), (sgb, b_sgu), (cvw, conv_w)):
                    sp.dma_start(dst[:], src[l]).then_inc(s_par, 16)
                for dst, g in ((g64[:, 0], g_qd), (g64[:, 1], g_kd), (g64[:, 2], g_qs), (g64[:, 3], g_ks), (gsv, g_sgu)):
                    sp.dma_start(dst[:], g[l].partition_broadcast(P)).then_inc(s_par, 16)

            def late_parameters(l):
                sp.dma_start(sgw[:], w_sgu[l]).then_inc(s_late, 16)
                sp.dma_start(gain_f[:], g_ffn[l].partition_broadcast(P)).then_inc(s_late, 16)
                sp.dma_start(sub[:], subkeys[l]).then_inc(s_late, 16)

            sp.dma_start(x[:, 0], x_in[0:P]).then_inc(s_x[0], 16)
            sp.dma_start(cst[:], cst_in).then_inc(s_cst, 16)
            parameters(0)
            for G, (s, i) in enumerate(PIECE_LIST):
                l = s // NC
                if (s, i) == (NC, 0):
                    sp.wait_ge(idx_ready, PH * s)
                    parameters(l)
                    late_parameters(l)
                if G == NB // 2:
                    late_parameters(0)
                    for c in range(1, NC):
                        sp.dma_start(x[:, c], x_in[c * P:(c + 1) * P]).then_inc(s_x[c], 16)
                place, there, _, used = piece_at(G)
                if used > 0:
                    sp.wait_ge(piece_ready, used)
                src = w_in[l, i] if i < N_IN else w_out[l, i - N_IN] if i < N_IN + N_OUT else w_q[l, i - N_IN - N_OUT]
                sp.dma_start(place, src).then_inc(there, 16)
            for c in range(NC):
                sp.wait_ge(x_done, STEPS - NC + c + 1)
                sp.dma_start(out[c * P:(c + 1) * P], x[:, c]).then_inc(s_out, 16)
            sp.wait_ge(s_out, 16 * NC)

        N_PAR, N_LATE = 9 * 16, 3 * 16

        @block.gpsimd
        def _(pool):
            for q, (kind, J, k) in enumerate(plan):
                s, h = divmod(J, PH)
                if kind == "u" and k == 0:
                    pool.wait_ge(idx_ready, TOP_NO[s, h] + 1)
                    if J == 0:
                        pool.wait_ge(piece_ready, W_EARLY)
                if q >= NB:
                    k0, J0, i0 = plan[q - NB]
                    if k0 == "u":
                        pool.wait_ge(dotted, TOPK * J0 + i0 + 1)
                    else:
                        by, m = V_NO[J0, i0]
                        pool.wait_ge(vx_used if by else v_used, m + 1)
                table = (tables_u if kind == "u" else tables_v)[s // NC]
                n = h * TOPK + k
                pool.indirect_dma_start(out=ring[:, q % NB], out_offset=None, in_=table,
                                        in_offset=bass.IndirectOffsetOnAxis(ap=idx[:, s % NS, n:n + 1], axis=0)
                                        ).then_inc(g_landed[q % NB], 16)

        def landed(eng, g):
            q = at[g]
            eng.wait_ge(g_landed[q % NB], 16 * (q // NB + 1))

        @block.scalar
        def _(act):
            made = [0]

            def link(ins):
                made[0] += 1
                ins.then_inc(act_chain, 1)
                act.wait_ge(act_chain, made[0])

            def take_batch(b, dst, width=512):
                act.wait_ge(tp_ready, b + 1)
                nc.scalar.activation(dst, psT[:, b % 2, :width], ACT.Copy).then_inc(tp_taken, 1)

            def row_sumsq(s):
                l, c = divmod(s, NC)
                link(nc.scalar.activation(sq[:], x[:, c], ACT.Square, accum_out=ss[:, 0:1]))
                act.sem_inc(sumsq, 1)

            def take_hT(part, s, first, gain):
                j, G = GROUP_OF[s].index(s), PIECE_NO[GROUP_OF[s][0], first]
                o = slice(j * P, (j + 1) * P)
                if G:
                    act.wait_ge(piece_ready, G)
                for b in range(2):
                    n = BATCH_NO[part, s, 0] + b
                    act.wait_ge(tp_ready, n + 1)
                    if gain is None:
                        last = nc.scalar.activation(hT[:, 4 * b:4 * b + 4, o],
                                                    psT[:, n % 2].rearrange("p (k t) -> p k t", t=P), ACT.Copy)
                    else:
                        for k in range(4):
                            last = nc.scalar.activation(hT[:, 4 * b + k, o], psT[:, n % 2, k * P:(k + 1) * P], ACT.Copy,
                                                        scale=gain_t[:, gain, 4 * b + k:4 * b + k + 1])
                    last.then_inc(tp_taken, 1)

            def front(s, part, i):
                l, c = divmod(s, NC)
                j = GROUP_OF[s].index(s)
                if part == "norm1":
                    act.wait_ge(s_x[c], 16)
                    if l:
                        act.wait_ge(x_done, s - NC + 1)
                    wait_for(act, hn_free("norm1", s))
                    row_sumsq(s)
                elif part == "hT1":
                    act.wait_ge(s_par, N_PAR * (l + 1))
                    take_hT("hT1", s, 0, 0)
                elif part == "piece":
                    G, n = PIECE_NO[s, i], len(GROUP_OF[s])
                    act.wait_ge(piece_ready, G + 1)
                    if i == 0 and s:
                        act.wait_ge(cat_sq, s)
                    src = psP[:, G % 2, :n * PW].rearrange("p (j w) -> p j w", j=n)
                    if i < 4:
                        dst = tm[:, :n, i]
                    elif i in (DV, BV):
                        dst = (vd if i == DV else vs)[:, c:c + n]
                        if l:
                            act.wait_ge(sb_out, NC * l)
                    elif i in (SU, SV):
                        dst = tm[:, :n, 4 + i - SU]
                    else:
                        src = psP[:, G % 2, :n * PW].rearrange("p (b j t) -> p b j t", b=2, j=n)
                        dst = fm[:, i - CB, :, :n]
                    nc.scalar.activation(dst, src, ACT.Gelu_apprx_tanh if i in (SU, SV) else ACT.Copy).then_inc(psp_act, 1)
                elif part == "qk squares":
                    wait_for(act, hn_free("qk", s))
                    act.wait_ge(*psp_freed(PIECE_NO[GROUP_OF[s][0], 3]))
                    nc.scalar.activation(sq[:], tm[:, j, 0:4].rearrange("p a b -> p (a b)"), ACT.Square).then_inc(qk_squared, 1)
                elif part == "qk taken":
                    for m, (dq, dk) in enumerate(((qdT, kdT), (qsT, ksT))):
                        n = BATCH_NO["qk", s, 0] + m
                        act.wait_ge(tp_ready, n + 1)
                        v = psT[:, n % 2].rearrange("p (a b) -> p a b", a=4)
                        nc.scalar.activation(dq[:, j], v[:, 0:2], ACT.Copy)
                        nc.scalar.activation(dk[:, :, c * P:(c + 1) * P], v[:, 2:4], ACT.Copy).then_inc(tp_taken, 1)
                elif part == "v squares":
                    wait_for(act, hn_free("sgu in", s))
                    act.wait_ge(*psp_freed(PIECE_NO[GROUP_OF[s][0], SV]))
                    nc.scalar.activation(sq[:, :MW], tm[:, j, 5], ACT.Square).then_inc(v_squared, 1)
                elif part == "dil exp":
                    w = (c + 1) * P
                    act.wait_ge(biased, H * s + i + 1)
                    nc.scalar.activation(prob[:, i % 2, :w], prob[:, i % 2, :w], ACT.Exp,
                                         bias=nmax[:, i:i + 1]).then_inc(expd, 1)
                elif part == "dil taken":
                    w = (c + 1) * P
                    if i >= 2:
                        act.wait_ge(dil_out, H * s + i - 1)
                    elif s:
                        act.wait_ge(sticked, uses_before(s))
                        act.wait_ge(sum_ready, uses_before(s))
                    take_batch(BATCH_NO["dil T", s, i], probT[:, i % 2, :w], w)
                elif part == "logits":
                    if i > c:
                        return
                    u = uses_before(s) + i
                    act.wait_ge(z_ready, u + 1)
                    if i == 0:
                        act.wait_ge(dil_out, H * (s + 1))
                    if i >= 2:
                        act.wait_ge(sticked, u - 1)
                        act.wait_ge(softed, u)
                        act.wait_ge(sum_ready, u - 1)
                    link(nc.scalar.activation(soft[:, u % 2], psS[:], ACT.Abs))
                    nc.scalar.activation(zs[:, u % 2], psS[:], ACT.Copy)
                    link(nc.scalar.activation(soft[:, u % 2], soft[:, u % 2], ACT.Exp, scale=-1.0))
                    nc.scalar.activation(soft[:, u % 2], soft[:, u % 2], ACT.Ln, bias=one).then_inc(z_taken, 1)
                elif part == "stick exp":
                    if i > c:
                        return
                    u = uses_before(s) + i
                    act.wait_ge(lesser, u + 1)
                    if s:
                        act.wait_ge(sb_out, s)
                    nc.scalar.activation(stick[:, c - i], zs[:, u % 2], ACT.Exp).then_inc(sticked, 1)
                elif part == "conv taken":
                    if s:
                        act.wait_ge(normed, NORMED_NO["cat", s - 1] + 1)
                    take_batch(BATCH_NO["conv", s, 0], cat[:, 2], MW)
                elif part == "cat squares":
                    act.wait_ge(cat_sq, s + 1)
                    wait_for(act, hn_free("cat", s))
                    nc.scalar.activation(sq[:], cat[:].rearrange("p a b -> p (a b)"), ACT.Square).then_inc(cat_squared, 1)
                elif part == "catT":
                    take_hT("catT", s, N_IN, 1)
                elif part == "norm2":
                    wait_for(act, hn_free("norm2", s))
                    act.wait_ge(x_mixed, s + 1)
                    row_sumsq(s)
                elif part == "hT2":
                    take_hT("hT2", s, N_IN + N_OUT, None)
                elif part == "queries":
                    G, n, Q = PIECE_NO[s, N_IN + N_OUT + i], len(GROUP_OF[s]), QUERY_NO[s, i]
                    act.wait_ge(piece_ready, G + 1)
                    if Q >= 2:
                        s0, h0 = list(QUERY_NO)[Q - 2]
                        act.wait_ge(s_scores, TOP_NO[GROUP_OF[s0][-1], h0] + 1)
                    nc.scalar.activation(qT[:, Q % 2, :, :n * P], psP[:, G % 2, :n * PW].rearrange("p (b t) -> p b t", b=2),
                                         ACT.Copy).then_inc(psp_act, 1)
                elif part == "key scores":
                    T = TOP_NO[s, i]
                    if T >= 2:
                        act.wait_ge(idx_ready, T - 1)
                    act.wait_ge(s_scores, T + 1)
                    nc.scalar.activation(sc[:, T % 2].rearrange("p a b -> p (a b)"), psS[:, :2 * P],
                                         ACT.Copy).then_inc(s_taken, 1)
                elif part == "gate exp":
                    T = TOP_NO[s, i]
                    act.wait_ge(idx_ready, T + 1)
                    if T:
                        act.wait_ge(gate_ready, T)
                    g = gate[:, s % NS, i * TOPK:(i + 1) * TOPK]
                    nc.scalar.activation(g, g, ACT.Exp, accum_out=gsum[:]).then_inc(top_exp, 1)

            for slot in range(FIRST_SLOT, 0):
                for part, s, i in at_slot("act", slot):
                    front(s, part, i)
            for J in range(HEADS + 1):
                for k in range(TOPK):
                    by, m = V_NO.get((J - 1, k), (1, 0))
                    if by == 0:
                        act.wait_ge(w_ready, J)
                        if m >= ND:
                            act.wait_ge(v_used, m - ND + 1)
                        nc.scalar.activation(diag[:, m % ND], ident, ACT.Copy,
                                             scale=wgt[:, (J - 1) % 2, k:k + 1]).then_inc(diag_ready, 1)
                    for part, s, i in at_slot("act", J * TOPK + k):
                        front(s, part, i)
                if J < HEADS:
                    act.wait_ge(dotted, TOPK * (J + 1))
                    if J:
                        act.wait_ge(w_ready, J)
                    nc.scalar.activation(gl[:], adot[:, J % PH * TOPK:(J % PH + 1) * TOPK],
                                         ACT.Gelu_apprx_tanh).then_inc(a_gelu, 1)

        @block.tensor
        def _(pe):
            def transposes(b, srcs):
                if b >= 2:
                    pe.wait_ge(tp_taken, b - 1)
                for i, src in enumerate(srcs):
                    last = nc.tensor.transpose(psT[:, b % 2, i * P:(i + 1) * P], src, ident)
                last.then_inc(tp_ready, 1)

            def project(s, i):
                G, n = PIECE_NO[s, i], len(GROUP_OF[s])
                w, there, value, _ = piece_at(G)
                pe.wait_ge(there, value)
                if G >= 2:
                    pe.wait_ge(*psp_freed(G - 2))
                bank = psP[:, G % 2]
                if CB <= i < N_IN or i >= N_IN + N_OUT:
                    for b in range(2):
                        for k in range(KD):
                            last = nc.tensor.matmul(bank[:, b * n * P:(b + 1) * n * P], w[:, k, b * P:(b + 1) * P],
                                                    hT[:, k, :n * P], start=(k == 0), stop=(k == KD - 1))
                else:
                    for j in range(n):
                        for k in range(KD):
                            last = nc.tensor.matmul(bank[:, j * PW:(j + 1) * PW], hT[:, k, j * P:(j + 1) * P], w[:, k],
                                                    start=(k == 0), stop=(k == KD - 1))
                last.then_inc(piece_ready, 1)

            def score(s, h):
                l, c = divmod(s, NC)
                j = GROUP_OF[s].index(s)
                if h == 0:
                    pe.wait_ge(tp_taken, BATCH_NO["qk", s, 0] + 2)
                wait_for(pe, pss_free("scores", s, h))
                r = slice(HD * (h % 2), HD * (h % 2) + HD)
                nc.tensor.matmul(psS[:, :(c + 1) * P], qdT[r, j, h // 2], kdT[r, h // 2, :(c + 1) * P],
                                 start=True, stop=True).then_inc(scored, 1)

            def logits(s, i):
                l, c = divmod(s, NC)
                u = uses_before(s) + i
                j = GROUP_OF[s].index(s)
                wait_for(pe, pss_free("logits", s, i))
                kc = c - i
                for h in (0, 2, 1, 3):
                    if h == 1:
                        last.then_inc(z_half, 1)
                        pe.wait_ge(z_half, u + 1)
                    r = slice(HD * (h % 2), HD * (h % 2) + HD)
                    last = nc.tensor.matmul(psS[:, h * P:(h + 1) * P], ksT[r, h // 2, kc * P:(kc + 1) * P],
                                            qsT[r, j, h // 2], start=True, stop=True)
                last.then_inc(z_ready, 1)

            def pso_wait(part, s, i):
                if PSO_NO[part, s, i]:
                    pe.wait_ge(pso_free, PSO_NO[part, s, i])

            def front(s, part, i):
                l, c = divmod(s, NC)
                j = GROUP_OF[s].index(s)
                if part in ("hT1", "catT", "hT2"):
                    n = NORMED_NO[{"hT1": "norm1", "catT": "cat", "hT2": "norm2"}[part], s]
                    pe.wait_ge(normed, n + 1)
                    for b in range(2):
                        transposes(BATCH_NO[part, s, 0] + b, [hn[:, (4 * b + k) * P:(4 * b + k + 1) * P] for k in range(4)])
                elif part == "piece":
                    if i in (0, N_IN, N_IN + N_OUT):
                        b = {0: "hT1", N_IN: "catT", N_IN + N_OUT: "hT2"}[i]
                        pe.wait_ge(tp_taken, BATCH_NO[b, GROUP_OF[s][-1], 0] + 2)
                    project(s, i)
                elif part == "qk":
                    pe.wait_ge(qk_done, s + 1)
                    for b in range(2):
                        transposes(BATCH_NO["qk", s, 0] + b, [hn[:, (4 * b + k) * P:(4 * b + k + 1) * P] for k in range(4)])
                elif part == "scores":
                    score(s, i)
                elif part == "dil T":
                    pe.wait_ge(weighed, H * s + i + 1)
                    transposes(BATCH_NO["dil T", s, i], [prob[:, i % 2, b * P:(b + 1) * P] for b in range(c + 1)])
                elif part == "dil out":
                    pe.wait_ge(tp_taken, BATCH_NO["dil T", s, i] + 1)
                    if i == 0:
                        pso_wait("dil out", s, 0)
                        pe.wait_ge(*psp_freed(PIECE_NO[GROUP_OF[s][0], DV]))
                    for j in range(c + 1):
                        last = nc.tensor.matmul(psO[:, i * HD:(i + 1) * HD], probT[:, i % 2, j * P:(j + 1) * P],
                                                vd[:, j, i * HD:(i + 1) * HD], start=(j == 0), stop=(j == c))
                    last.then_inc(dil_out, 1)
                elif part == "logits":
                    if i <= c:
                        logits(s, i)
                elif part == "sums":
                    u = uses_before(s) + i
                    pe.wait_ge(softed, u + 1)
                    pso_wait("sums", s, i)
                    last = nc.tensor.matmul(psO[:], cst[:, C_TRI:C_TRI + P], soft[:, u % 2], start=True, stop=(i == 0))
                    if i:
                        last = nc.tensor.matmul(psO[:], cst[:, C_ONE:C_ONE + P], later[:], start=False, stop=True)
                    last.then_inc(sum_ready, 1)
                elif part == "stick out":
                    pe.wait_ge(sticked, uses_before(s + 1))
                    pso_wait("stick out", s, 0)
                    for h in range(H):
                        for j in range(c + 1):
                            last = nc.tensor.matmul(psO[:, h * HD:(h + 1) * HD], stick[:, j, h * P:(h + 1) * P],
                                                    vs[:, j, h * HD:(h + 1) * HD], start=(j == 0), stop=(j == c))
                    last.then_inc(sb_out, 1)
                elif part == "sgu":
                    pe.wait_ge(sgu_in, s + 1)
                    pso_wait("sgu", s, 0)
                    for h in range(H):
                        last = nc.tensor.matmul(psO[:, h * HD:(h + 1) * HD], sgw[:, h], tm[:, j, 5, h * HD:(h + 1) * HD],
                                                start=True, stop=True)
                    last.then_inc(sgu_out, 1)
                elif part == "conv":
                    pe.wait_ge(conv_done, s + 1)
                    transposes(BATCH_NO["conv", s, 0], [cv[:, 0], cv[:, 1]])
                elif part == "key scores":
                    a = GROUP_OF[s][0]
                    pe.wait_ge(s_late, N_LATE * (l + 1))
                    pe.wait_ge(*psp_freed(PIECE_NO[a, N_IN + N_OUT + i]))
                    wait_for(pe, pss_free("key scores", s, i))
                    for b in range(2):
                        last = nc.tensor.matmul(psS[:, b * P:(b + 1) * P], qT[:, QUERY_NO[a, i] % 2, b, j * P:(j + 1) * P],
                                                sub[:, 2 * i + b], start=True, stop=True)
                    last.then_inc(s_scores, 1)

            pe.wait_ge(s_cst, 16)
            for slot in range(FIRST_SLOT, 0):
                for part, s, i in at_slot("pe", slot):
                    front(s, part, i)
            for J in range(HEADS + 1):
                for k in range(TOPK):
                    by, m = V_NO.get((J - 1, k), (1, 0))
                    if by == 0:
                        s, h = divmod(J - 1, PH)
                        first, final = m == v_rows(PH * s, 0), m == v_rows(PH * (s + 1), 0) - 1
                        landed(pe, ("v", J - 1, k))
                        pe.wait_ge(diag_ready, m + 1)
                        if first and s:
                            pe.wait_ge(x_done, s)
                        r = ring[:, at[("v", J - 1, k)] % NB]
                        for b in range(2):
                            last = nc.tensor.matmul(psY[:, b * 512:(b + 1) * 512], diag[:, m % ND],
                                                    r[:, b * 512:(b + 1) * 512], start=first, stop=final)
                        last.then_inc(v_used, 1)
                    for part, s, i in at_slot("pe", J * TOPK + k):
                        front(s, part, i)

        @block.vector
        def _(dve):
            v = nc.vector
            made = [0]

            def link(ins):
                after(mark(ins))

            def mark(ins):
                made[0] += 1
                ins.then_inc(dve_chain, 1)
                return made[0]

            def after(number):
                dve.wait_ge(dve_chain, number)

            def root(n, width, terms):
                m, r, t, u = ss[:, :width], rs[:, :width], nt[:, 0, :width], nt[:, 1, :width]
                dve.wait_ge(sumsq, n)
                link(v.tensor_scalar(t, m, 1.0 / terms, EPS, ALU.mult, ALU.add))
                link(v.tensor_scalar(r.bitcast(I32), t.bitcast(I32), -0.5, float(ROOT_MAGIC), ALU.mult, ALU.add))
                for _ in range(NEWTON):
                    link(v.scalar_tensor_tensor(out=u, in0=r, scalar=-0.5, in1=r, op0=ALU.mult, op1=ALU.mult))
                    link(v.tensor_tensor(u, u, t, ALU.mult))
                    link(v.scalar_tensor_tensor(out=r, in0=u, scalar=1.5, in1=r, op0=ALU.add, op1=ALU.mult))

            def per_head(t, heads):
                return t[:, :heads].unsqueeze(2).broadcast_to([P, heads, HD])

            def top16(lists):
                first = [mark(v.max(values[:, 0:8], src)) for src, values, _, _ in lists]
                rest = []
                for m, (src, values, places, scratch) in zip(first, lists):
                    after(m)
                    rest.append(mark(v.match_replace(scratch, values[:, 0:8], src, LOWEST)))
                    mark(v.max_index(places[:, 0:8], values[:, 0:8], src))
                last = []
                for m, (src, values, places, scratch) in zip(rest, lists):
                    after(m)
                    last.append(mark(v.max(values[:, 8:16], scratch)))
                for m, (src, values, places, scratch) in zip(last, lists):
                    after(m)
                    found = mark(v.max_index(places[:, 8:16], values[:, 8:16], scratch))
                return found

            def across_heads(o):
                return cst[:, o:o + P].unsqueeze(1).broadcast_to([P, H, P])

            def front(s, part, i):
                l, c = divmod(s, NC)
                j = GROUP_OF[s].index(s)
                n = NORM_NO.get((part, s), 0) + 1
                if part == "norm1":
                    if c == 0:
                        dve.wait_ge(s_par, N_PAR * (l + 1))
                    root(n, 1, D)
                    v.tensor_scalar(hn[:], x[:, c], rs[:, 0:1], None, ALU.mult).then_inc(normed, 1)
                elif part == "qk":
                    dve.wait_ge(qk_squared, s + 1)
                    v.tensor_reduce(ss[:], sq[:].rearrange("p (h d) -> p h d", d=HD), AX.X, ALU.add).then_inc(sumsq, 1)
                    root(n, 16, HD)
                    hv = hn[:].rearrange("p (h d) -> p h d", d=HD)
                    link(v.tensor_tensor(hv, tm[:, j, 0:4].rearrange("p a (h d) -> p (a h) d", d=HD), per_head(rs, 16), ALU.mult))
                    h4 = hn[:].rearrange("p (a h d) -> p a h d", a=4, d=HD)
                    link(v.tensor_tensor(h4, h4, g64[:].unsqueeze(2).broadcast_to([P, 4, H, HD]), ALU.mult))
                    q = hn[:].rearrange("p (a b c) -> p a b c", a=2, b=2)[:, :, 0]
                    v.tensor_scalar(q, q, HD ** -0.5, None, ALU.mult).then_inc(qk_done, 1)
                elif part == "bias":
                    w, N = (c + 1) * P, H * s + i
                    pr = prob[:, i % 2, :w]
                    o = C_DELTA + (NC - 1 - c) * P
                    if i == 0 and s:
                        dve.wait_ge(sticked, uses_before(s))
                    if i >= 2:
                        dve.wait_ge(tp_ready, BATCH_NO["dil T", s, i - 2] + 1)
                    dve.wait_ge(scored, N + 1)
                    link(v.scalar_tensor_tensor(out=pr, in0=cst[:, o:o + w], scalar=-SLOPES[i], in1=psS[:, :w],
                                                op0=ALU.mult, op1=ALU.add))
                    v.tensor_reduce(nmax[:, i:i + 1], pr, AX.X, ALU.max, negate=True).then_inc(biased, 1)
                elif part == "weigh":
                    w, N = (c + 1) * P, H * s + i
                    pr = prob[:, i % 2, :w]
                    dve.wait_ge(expd, N + 1)
                    o = C_MULT + (NC - 1 - c) * P
                    v.tensor_tensor_reduce(out=pr, in0=pr, in1=cst[:, o:o + w], scale=1.0, scalar=0.0, op0=ALU.mult,
                                           op1=ALU.add, accum_out=den[:, i:i + 1]).then_inc(weighed, 1)
                elif part == "dil out":
                    dve.wait_ge(weighed, H * (s + 1))
                    link(v.reciprocal(rden[:], den[:]))
                    dve.wait_ge(dil_out, H * (s + 1))
                    if s:
                        dve.wait_ge(cat_squared, s)
                    v.tensor_tensor(cat[:, 1].rearrange("p (h d) -> p h d", d=HD),
                                    psO[:, :MW].rearrange("p (h d) -> p h d", d=HD), per_head(rden, H),
                                    ALU.mult).then_inc(pso_free, 1)
                elif part == "softplus":
                    u = uses_before(s) + i
                    z, f = zs[:, u % 2], soft[:, u % 2]
                    dve.wait_ge(z_taken, u + 1)
                    if i == 1:
                        if s:
                            dve.wait_ge(sum_ready, u)
                        link(v.tensor_copy(later[:], soft[:, (u - 1) % 2]))
                    elif i > 1:
                        dve.wait_ge(sum_ready, u)
                        link(v.tensor_tensor(later[:], later[:], soft[:, (u - 1) % 2], ALU.add))
                    ins = v.scalar_tensor_tensor(out=f, in0=z, scalar=0.0, in1=f, op0=ALU.max, op1=ALU.add)
                    if i == 0:
                        link(ins)
                        fm4 = f.rearrange("p (h q) -> p h q", q=P)
                        ins = v.tensor_tensor(fm4, fm4, across_heads(C_STRICT), ALU.mult)
                    ins.then_inc(softed, 1)
                elif part == "exponent":
                    u = uses_before(s) + i
                    z = zs[:, u % 2]
                    dve.wait_ge(sum_ready, u + 1)
                    v.tensor_tensor(z, z, psO[:], ALU.subtract).then_inc(pso_free, 1)
                    dve.wait_ge(pso_free, PSO_NO["sums", s, i] + 1)
                    if i == 0:
                        link(v.tensor_scalar(z, z, 0.0, None, ALU.min))
                        z4 = z.rearrange("p (h q) -> p h q", q=P)
                        v.tensor_tensor(z4, z4, across_heads(C_NEG), ALU.add).then_inc(lesser, 1)
                    else:
                        v.tensor_scalar(z, z, 0.0, None, ALU.min).then_inc(lesser, 1)
                elif part == "stick out":
                    dve.wait_ge(sb_out, s + 1)
                    v.tensor_copy(cat[:, 3], psO[:, :MW]).then_inc(pso_free, 1)
                elif part == "sgu in":
                    if c == 0:
                        dve.wait_ge(s_late, N_LATE * (l + 1))
                        mark(v.tensor_tensor(sgw[:], sgw[:], across_heads(C_TRIL), ALU.mult))
                    dve.wait_ge(v_squared, s + 1)
                    v.tensor_reduce(ss[:, :H], sq[:, :MW].rearrange("p (h d) -> p h d", d=HD), AX.X, ALU.add).then_inc(sumsq, 1)
                    root(n, H, HD)
                    vv = tm[:, j, 5].rearrange("p (h d) -> p h d", d=HD)
                    link(v.tensor_tensor(vv, vv, per_head(rs, H), ALU.mult))
                    v.tensor_tensor(tm[:, j, 5], tm[:, j, 5], gsv[:], ALU.mult).then_inc(sgu_in, 1)
                elif part == "sgu":
                    dve.wait_ge(sgu_out, s + 1)
                    for h in range(H):
                        o = slice(h * HD, (h + 1) * HD)
                        last = v.scalar_tensor_tensor(out=cat[:, 0, o], in0=psO[:, o], scalar=sgb[:, h:h + 1],
                                                      in1=tm[:, j, 4, o], op0=ALU.add, op1=ALU.mult)
                    last.then_inc(pso_free, 1)
                elif part == "conv":
                    dve.wait_ge(*psp_freed(PIECE_NO[GROUP_OF[s][0], N_IN - 1]))
                    if c == 0:
                        link(v.memset(yc[:, :, 0:2], 0.0))
                    else:
                        link(v.tensor_copy(yc[:, :, 0:2], yc[:, :, P:P + 2]))
                    link(v.tensor_tensor(yc[:, :, 2:], fm[:, 1, :, j], fm[:, 2, :, j], ALU.mult))
                    if s:
                        dve.wait_ge(tp_ready, BATCH_NO["conv", s - 1, 0] + 1)
                    for b in range(2):
                        link(v.tensor_scalar(cv[:, b], yc[:, b, 0:P], cvw[:, b, 0:1], None, ALU.mult))
                        for t in (1, 2):
                            link(v.scalar_tensor_tensor(out=cv[:, b], in0=yc[:, b, t:t + P], scalar=cvw[:, b, t:t + 1],
                                                        in1=cv[:, b], op0=ALU.mult, op1=ALU.add))
                    v.tensor_tensor(cv[:], cv[:], fm[:, 0, :, j], ALU.mult).then_inc(conv_done, 1)
                elif part == "cat":
                    dve.wait_ge(cat_squared, s + 1)
                    v.tensor_reduce(ss[:], sq[:].rearrange("p (h d) -> p h d", d=HD), AX.X, ALU.add).then_inc(sumsq, 1)
                    root(n, 16, HD)
                    hv = hn[:].rearrange("p (h d) -> p h d", d=HD)
                    v.tensor_tensor(hv, cat[:].rearrange("p a (h d) -> p (a h) d", d=HD), per_head(rs, 16),
                                    ALU.mult).then_inc(normed, 1)
                elif part == "out":
                    G, n = PIECE_NO[s, N_IN + i], len(GROUP_OF[s])
                    dve.wait_ge(piece_ready, G + 1)
                    xs = x[:, c:c + n, i * PW:(i + 1) * PW]
                    v.tensor_tensor(xs, xs, psP[:, G % 2, :n * PW].rearrange("p (j w) -> p j w", j=n),
                                    ALU.add).then_inc(psp_dve, 1)
                elif part == "norm2":
                    root(n, 1, D)
                    if s >= NS:
                        dve.wait_ge(dotted, SLOTS * (s - NS + 1))
                    link(v.scalar_tensor_tensor(out=htok[:, s % NS], in0=x[:, c], scalar=rs[:, 0:1], in1=gain_f[:],
                                                op0=ALU.mult, op1=ALU.mult))
                    v.tensor_copy(hn[:], htok[:, s % NS]).then_inc(normed, 1)
                elif part == "top keys":
                    T = TOP_NO[s, i]
                    dve.wait_ge(s_taken, T + 1)
                    if T:
                        dve.wait_ge(idx_ready, T)
                    after(top16([(sc[:, T % 2, b], sv[:, b], si[:, b], sc2[:, b * P:(b + 1) * P]) for b in range(2)]))
                elif part == "top pairs":
                    if i == 0 and s >= NS:
                        dve.wait_ge(v_used, v_rows(PH * (s - NS + 1), 0))
                        dve.wait_ge(vx_used, v_rows(PH * (s - NS + 1), 1))
                    o = slice(i * TOPK, (i + 1) * TOPK)
                    link(v.tensor_tensor(cand[:], sv[:, 0].unsqueeze(2).broadcast_to([P, TOPK, TOPK]),
                                         sv[:, 1].unsqueeze(1).broadcast_to([P, TOPK, TOPK]), ALU.add))
                    found = top16([(cand[:].rearrange("p a b -> p (a b)"), top, pos[:, 0], sc2[:])])
                    mark(v.tensor_scalar(gate[:, s % NS, o], top[:], top[:, 0:1], None, ALU.subtract))
                    after(found)
                    mark(v.tensor_scalar(pos[:, 1], pos[:, 0], 4, None, ALU.logical_shift_right))
                    link(v.tensor_scalar(pos[:, 2], pos[:, 0], 15, None, ALU.bitwise_and))
                    shape = [P, 2, TOPK, TOPK]
                    iota = cst[:, C_IOTA:C_IOTA + TOPK].unsqueeze(1).unsqueeze(1).broadcast_to(shape)
                    link(v.tensor_tensor(hot[:], pos[:, 1:3].unsqueeze(3).broadcast_to(shape), iota, ALU.is_equal))
                    link(v.tensor_tensor(hot[:], hot[:], si[:].unsqueeze(2).broadcast_to(shape), ALU.mult))
                    link(v.tensor_reduce(pick[:], hot[:], AX.X, ALU.add))
                    v.scalar_tensor_tensor(out=idx[:, s % NS, o], in0=pick[:, 0], scalar=float(P), in1=pick[:, 1],
                                           op0=ALU.mult, op1=ALU.add).then_inc(idx_ready, 1)
                elif part == "gate":
                    dve.wait_ge(top_exp, TOP_NO[s, i] + 1)
                    g = gate[:, s % NS, i * TOPK:(i + 1) * TOPK]
                    link(v.reciprocal(rsum[:], gsum[:]))
                    v.tensor_scalar(g, g, rsum[:], None, ALU.mult).then_inc(gate_ready, 1)

                if part == "stick out":
                    dve.wait_ge(tp_taken, BATCH_NO["conv", s, 0] + 1)
                    dve.wait_ge(pso_free, PSO_NO["stick out", s, 0] + 1)
                    dve.sem_inc(cat_sq, 1)
                if part == "out" and i == N_OUT - 1:
                    dve.wait_ge(psp_dve, psp_freed(PIECE_NO[s, N_IN + i])[1])
                    dve.sem_inc(x_mixed, len(GROUP_OF[s]))

            def add_peer(s):
                dve.wait_ge(v_used, v_rows(PH * (s + 1), 0))
                dve.wait_ge(vx_used, v_rows(PH * (s + 1), 1))
                v.tensor_tensor(x[:, s % NC], x[:, s % NC], psY[:], ALU.add).then_inc(x_done, 1)

            dve.wait_ge(s_cst, 16)
            for slot in range(FIRST_SLOT, 0):
                for part, s, i in at_slot("dve", slot):
                    front(s, part, i)
            for J in range(HEADS + 1):
                s, h = divmod(J, PH)
                for k in range(TOPK):
                    if J < HEADS:
                        n = h * TOPK + k
                        landed(dve, ("u", J, k))
                        r = ring[:, at[("u", J, k)] % NB]
                        v.tensor_tensor_reduce(out=r, in0=r, in1=htok[:, s % NS], scale=1.0, scalar=0.0,
                                               op0=ALU.mult, op1=ALU.add, accum_out=adot[:, n:n + 1]).then_inc(dotted, 1)
                    by, m = V_NO.get((J - 1, k), (0, 0))
                    if by:
                        xs = x[:, (J - 1) // PH % NC]
                        landed(dve, ("v", J - 1, k))
                        dve.wait_ge(w_ready, J)
                        if m:
                            dve.wait_ge(vx_used, m)
                        v.scalar_tensor_tensor(out=xs, in0=ring[:, at[("v", J - 1, k)] % NB],
                                               scalar=wgt[:, (J - 1) % 2, k:k + 1], in1=xs,
                                               op0=ALU.mult, op1=ALU.add).then_inc(vx_used, 1)
                    for part, s1, i in at_slot("dve", J * TOPK + k):
                        front(s1, part, i)
                if J < HEADS:
                    dve.wait_ge(gate_ready, TOP_NO[s, h] + 1)
                    dve.wait_ge(a_gelu, J + 1)
                    if J >= 2:
                        dve.wait_ge(diag_ready, v_rows(J - 1, 0))
                    v.tensor_tensor(wgt[:, J % 2], gl[:], gate[:, s % NS, h * TOPK:(h + 1) * TOPK], ALU.mult).then_inc(w_ready, 1)
                if J >= PH and J % PH == 0:
                    add_peer(J // PH - 1)


def kernel(x, g_mix_norm, w_in, w_sgu, b_sgu, g_sgu_v, g_q_dil, g_k_dil, conv_w, g_q_sb, g_k_sb, g_head_out,
           w_out, g_ffn_norm, w_peer_q, peer_sub_keys, peer_u, peer_v):
    import concourse.bacc as bacc
    from concourse.bass_utils import run_bass_kernel_spmd

    def pieces(w):
        w = np.asarray(w)
        return w.reshape(DEPTH, KD, P, -1, PW).transpose(0, 3, 2, 1, 4)

    ins = {
        "x": np.asarray(x).reshape(SEQ, D),
        "cst": constants(),
        "w_in": pieces(w_in)[:, IN_ORDER],
        "w_out": pieces(w_out),
        "w_q": pieces(w_peer_q),
        "subkeys": np.asarray(peer_sub_keys).reshape(DEPTH, 2 * PH, P, P).transpose(0, 3, 1, 2),
        "w_sgu": np.asarray(w_sgu).transpose(0, 3, 1, 2),
        "b_sgu": np.asarray(b_sgu).transpose(0, 2, 1),
        "conv_w": np.asarray(conv_w).reshape(DEPTH, 3, 2, P).transpose(0, 3, 2, 1),
        "g_mix": np.asarray(g_mix_norm).reshape(DEPTH, KD, P).transpose(0, 2, 1),
        "g_head": np.asarray(g_head_out).reshape(DEPTH, KD, P).transpose(0, 2, 1),
        "g_ffn": np.asarray(g_ffn_norm),
        "g_sgu": np.asarray(g_sgu_v), "g_qd": np.asarray(g_q_dil), "g_kd": np.asarray(g_k_dil),
        "g_qs": np.asarray(g_q_sb), "g_ks": np.asarray(g_k_sb),
        "u0": np.asarray(peer_u)[0], "u1": np.asarray(peer_u)[1],
        "v0": np.asarray(peer_v)[0], "v1": np.asarray(peer_v)[1],
    }
    nc = bacc.Bacc("TRN2", target_bir_lowering=False, num_devices=1)
    arrays, args = {}, []
    for name, a in ins.items():
        a = np.ascontiguousarray(a)
        arrays["in_" + name] = a
        args.append(nc.dram_tensor("in_" + name, a.shape, mybir.dt.from_np(a.dtype), kind="ExternalInput").ap())
    args.append(nc.dram_tensor("out", (SEQ, D), F32, kind="ExternalOutput").ap())
    trunk(nc, *args)
    r = run_bass_kernel_spmd(nc, [arrays], core_ids=[0])
    return r.results[0]["out"].reshape(1, SEQ, D)
```
